# Optimizing a Trainium2 kernel written in Bass

```python
import jax, jax.numpy as jnp
from jax import lax
import numpy as np

D_MODEL = 2048
BATCH = 1
SEQ = 256
DEPTH = 2

N_EVEN = (DEPTH + 1) // 2
N_ODD = DEPTH // 2

HEAD_DIM = 128
NSA_HEADS = D_MODEL // (2 * HEAD_DIM)
NSA_KV_HEADS = max(1, NSA_HEADS // 4)
NSA_GROUP = NSA_HEADS // NSA_KV_HEADS
NSA_WIDTH = NSA_HEADS * HEAD_DIM
KV_WIDTH = NSA_KV_HEADS * HEAD_DIM
N_BRANCH = 3
CMP_BLOCK = 32
CMP_STRIDE = 16
SLC_BLOCK = 64
N_SLC = 16
N_LOCAL_SLC = 2
WINDOW = 512
WIN_Q_BLOCK = 128
SEL_Q_BLOCK = 64
FORCE_SCORE = 1e9

GMLP_GROUP_DIM = 128
GMLP_GROUPS = D_MODEL // (2 * GMLP_GROUP_DIM)
GMLP_WIDTH = GMLP_GROUPS * GMLP_GROUP_DIM
GMLP_CHUNK = 128

EVEN_SPLITS = [NSA_WIDTH] + [KV_WIDTH] * 6 + [N_BRANCH * NSA_HEADS, GMLP_WIDTH, GMLP_WIDTH]
EVEN_IN_WIDTH = sum(EVEN_SPLITS)
MIX_OUT_WIDTH = NSA_WIDTH + GMLP_WIDTH

CONV_WIDTH = 3
SCONV_WIDTH = D_MODEL

D_FF = ((8 * D_MODEL // 3) + 255) // 256 * 256

EPS = 1e-6
NEG = -1e30

kernel_name = "hybrid_nsa_gmlp_shortconv_convffn"

def rms_norm(x, g):
    xf = x.astype(jnp.float32)
    y = xf * lax.rsqrt(jnp.mean(xf * xf, axis=-1, keepdims=True) + EPS)
    return (y * g.astype(jnp.float32)).astype(x.dtype)

def layer_norm(x, g):
    xf = x.astype(jnp.float32)
    xc = xf - jnp.mean(xf, axis=-1, keepdims=True)
    y = xc * lax.rsqrt(jnp.mean(xc * xc, axis=-1, keepdims=True) + EPS)
    return (y * g.astype(jnp.float32)).astype(x.dtype)

def causal_dwconv3(x, w):
    s = x.shape[1]
    xp = jnp.pad(x, ((0, 0), (CONV_WIDTH - 1, 0), (0, 0)))
    return w[0] * xp[:, 0:s] + w[1] * xp[:, 1:s + 1] + w[2] * xp[:, 2:s + 2]

def masked_softmax(s, mask):
    s = jnp.where(mask, s.astype(jnp.float32), NEG)
    m = jnp.max(s, axis=-1, keepdims=True)
    p = jnp.exp(s - m) * mask
    return p / jnp.maximum(jnp.sum(p, axis=-1, keepdims=True), 1e-30)

def nsa_mixer(q, k_cmp, v_cmp, k_slc, v_slc, k_win, v_win, gate_logits,
              q_gain, k_gain, cmp_pe, cmp_k_w1, cmp_k_w2, cmp_v_w1, cmp_v_w2):
    b_, s, _, d = q.shape
    g_, r_ = NSA_KV_HEADS, NSA_GROUP
    pos = jnp.arange(s)
    qg = (rms_norm(q, q_gain) * (d ** -0.5)).reshape(b_, s, g_, r_, d)

    n_cmp = (s - CMP_BLOCK) // CMP_STRIDE + 1
    blk_idx = jnp.arange(n_cmp)[:, None] * CMP_STRIDE + jnp.arange(CMP_BLOCK)[None, :]

    def compress(kv, w1, w2):
        blocks = kv[:, blk_idx] + cmp_pe[:, None, :]
        h = jax.nn.gelu(jnp.einsum('bnlgd,lde->bnge', blocks, w1))
        return jnp.einsum('bnge,ef->bngf', h, w2)

    kc = rms_norm(compress(k_cmp, cmp_k_w1, cmp_k_w2), k_gain[0])
    vc = compress(v_cmp, cmp_v_w1, cmp_v_w2)
    cmp_end = jnp.arange(n_cmp) * CMP_STRIDE + CMP_BLOCK - 1
    cmp_mask = cmp_end[None, :] <= pos[:, None]
    p_cmp = masked_softmax(jnp.einsum('bsgrd,bngd->bgrsn', qg, kc), cmp_mask)
    o_cmp = jnp.einsum('bgrsn,bngd->bsgrd', p_cmp.astype(vc.dtype), vc)

    n_slc = s // SLC_BLOCK
    n_top = min(N_SLC, n_slc)
    cs = jnp.arange(n_cmp) * CMP_STRIDE
    ss = jnp.arange(n_slc) * SLC_BLOCK
    overlap = ((cs[:, None] < ss[None, :] + SLC_BLOCK) &
               (cs[:, None] + CMP_BLOCK > ss[None, :])).astype(jnp.float32)
    imp = jnp.einsum('bgrsn,nj->bgsj', p_cmp, overlap)
    jb = jnp.arange(n_slc)
    cur = pos // SLC_BLOCK
    causal_blk = ss[None, :] <= pos[:, None]
    forced = (jb[None, :] == 0) | ((cur[:, None] - jb[None, :] >= 0) &
                                   (cur[:, None] - jb[None, :] < N_LOCAL_SLC))
    imp = jnp.where(causal_blk, imp, NEG)
    imp = jnp.where(forced, FORCE_SCORE, imp)
    _, sel = lax.top_k(imp, n_top)

    kb = rms_norm(k_slc, k_gain[1]).reshape(b_, n_slc, SLC_BLOCK, g_, d).transpose(0, 3, 1, 2, 4)
    vb = v_slc.reshape(b_, n_slc, SLC_BLOCK, g_, d).transpose(0, 3, 1, 2, 4)
    nq = s // SEL_Q_BLOCK
    q_blocks = qg.reshape(b_, nq, SEL_Q_BLOCK, g_, r_, d).transpose(1, 0, 3, 4, 2, 5)
    sel_blocks = sel.reshape(b_, g_, nq, SEL_Q_BLOCK, n_top).transpose(2, 0, 1, 3, 4)
    bi = jnp.arange(b_)[:, None, None, None]
    gi = jnp.arange(g_)[None, :, None, None]
    n_keys = n_top * SLC_BLOCK

    def sel_block(args):
        qb, idx, start = args
        kg = kb[bi, gi, idx].reshape(b_, g_, SEL_Q_BLOCK, n_keys, d)
        vg = vb[bi, gi, idx].reshape(b_, g_, SEL_Q_BLOCK, n_keys, d)
        kpos = (idx[..., None] * SLC_BLOCK + jnp.arange(SLC_BLOCK)).reshape(b_, g_, SEL_Q_BLOCK, n_keys)
        qpos = start + jnp.arange(SEL_Q_BLOCK)
        mask = kpos[:, :, None] <= qpos[None, None, None, :, None]
        p = masked_softmax(jnp.einsum('bgrqd,bgqkd->bgrqk', qb, kg), mask)
        return jnp.einsum('bgrqk,bgqkd->bgrqd', p.astype(vg.dtype), vg)

    o_slc = lax.map(sel_block, (q_blocks, sel_blocks, jnp.arange(nq) * SEL_Q_BLOCK))
    o_slc = o_slc.transpose(1, 0, 4, 2, 3, 5).reshape(b_, s, g_, r_, d)

    nw = s // WIN_Q_BLOCK
    n_prev = WINDOW // WIN_Q_BLOCK
    kband = (n_prev + 1) * WIN_Q_BLOCK
    pad = ((0, 0), (WINDOW, 0), (0, 0), (0, 0))
    kp = jnp.pad(rms_norm(k_win, k_gain[2]), pad).reshape(b_, nw + n_prev, WIN_Q_BLOCK, g_, d)
    vp = jnp.pad(v_win, pad).reshape(b_, nw + n_prev, WIN_Q_BLOCK, g_, d)
    k_band = jnp.concatenate([kp[:, j:j + nw] for j in range(n_prev + 1)], axis=2)
    v_band = jnp.concatenate([vp[:, j:j + nw] for j in range(n_prev + 1)], axis=2)
    q_w = qg.reshape(b_, nw, WIN_Q_BLOCK, g_, r_, d)
    c0 = jnp.arange(nw)[:, None, None] * WIN_Q_BLOCK
    qpos_w = c0 + jnp.arange(WIN_Q_BLOCK)[None, :, None]
    kpos_w = c0 - WINDOW + jnp.arange(kband)[None, None, :]
    win_mask = (kpos_w >= 0) & (kpos_w <= qpos_w) & (qpos_w - kpos_w < WINDOW)
    p_win = masked_softmax(jnp.einsum('bcqgrd,bckgd->bgrcqk', q_w, k_band), win_mask)
    o_win = jnp.einsum('bgrcqk,bckgd->bcqgrd', p_win.astype(v_band.dtype), v_band).reshape(b_, s, g_, r_, d)

    gates = jax.nn.sigmoid(gate_logits).reshape(b_, s, g_, r_, N_BRANCH)
    o = gates[..., 0:1] * o_cmp + gates[..., 1:2] * o_slc + gates[..., 2:3] * o_win
    return o.reshape(b_, s, NSA_WIDTH)

def gmlp_mixer(uv, v_gain, w_s, b_s):
    b_, s, _ = uv.shape
    z = jax.nn.gelu(uv)
    u, v = z[..., :GMLP_WIDTH], z[..., GMLP_WIDTH:]
    v = layer_norm(v.reshape(b_, s, GMLP_GROUPS, GMLP_GROUP_DIM), v_gain)
    nc = s // GMLP_CHUNK
    vc = v.reshape(b_, nc, GMLP_CHUNK, GMLP_GROUPS, GMLP_GROUP_DIM)
    w = w_s * jnp.tril(jnp.ones((GMLP_CHUNK, GMLP_CHUNK), w_s.dtype))
    mixed = jnp.einsum('gts,bcsgd->bctgd', w, vc) + b_s.T[None, None, :, :, None]
    return u * mixed.reshape(b_, s, GMLP_WIDTH)

def even_mixer(x, norm_g, w_in, q_gain, k_gain, cmp_pe, cmp_k_w1, cmp_k_w2, cmp_v_w1, cmp_v_w2,
               gmlp_norm, gmlp_ws, gmlp_b, w_out):
    b_, s, _ = x.shape
    p = rms_norm(x, norm_g) @ w_in
    q, kc, vc, ks, vs, kw, vw, gl, uv_u, uv_v = jnp.split(p, list(np.cumsum(EVEN_SPLITS)[:-1]), axis=-1)
    kv = lambda t: t.reshape(b_, s, NSA_KV_HEADS, HEAD_DIM)
    o_a = nsa_mixer(q.reshape(b_, s, NSA_HEADS, HEAD_DIM), kv(kc), kv(vc), kv(ks), kv(vs), kv(kw), kv(vw),
                    gl.reshape(b_, s, NSA_HEADS, N_BRANCH), q_gain, k_gain, cmp_pe,
                    cmp_k_w1, cmp_k_w2, cmp_v_w1, cmp_v_w2)
    o_b = gmlp_mixer(jnp.concatenate([uv_u, uv_v], axis=-1), gmlp_norm, gmlp_ws, gmlp_b)
    return jnp.concatenate([o_a, o_b], axis=-1) @ w_out

def odd_mixer(x, norm_g, w_in, conv_w, w_out):
    bg, cg, xt = jnp.split(rms_norm(x, norm_g) @ w_in, 3, axis=-1)
    return (bg * causal_dwconv3(cg * xt, conv_w)) @ w_out

def conv_ffn(x, norm_g, w_in, conv_w, conv_b, w_down):
    g, u = jnp.split(rms_norm(x, norm_g) @ w_in, 2, axis=-1)
    g = causal_dwconv3(g, conv_w) + conv_b
    return (jax.nn.silu(g) * u) @ w_down

def setup_inputs(seed: int = 0) -> dict:
    key = jax.random.key(seed)
    ks = iter(jax.random.split(key, 32))

    def nrm(shape, scale):
        return jax.random.normal(next(ks), shape, jnp.float32) * scale

    def gain(shape):
        return 1.0 + nrm(shape, 0.02)

    d = HEAD_DIM
    return {
        "x": nrm((BATCH, SEQ, D_MODEL), 1.0),
        "ev_norm": gain((N_EVEN, D_MODEL)),
        "ev_w_in": nrm((N_EVEN, D_MODEL, EVEN_IN_WIDTH), D_MODEL ** -0.5),
        "ev_q_gain": gain((N_EVEN, d)),
        "ev_k_gain": gain((N_EVEN, N_BRANCH, d)),
        "ev_cmp_pe": nrm((N_EVEN, CMP_BLOCK, d), 0.2),
        "ev_cmp_k_w1": nrm((N_EVEN, CMP_BLOCK, d, d), (CMP_BLOCK * d) ** -0.5),
        "ev_cmp_k_w2": nrm((N_EVEN, d, d), d ** -0.5),
        "ev_cmp_v_w1": nrm((N_EVEN, CMP_BLOCK, d, d), (CMP_BLOCK * d) ** -0.5),
        "ev_cmp_v_w2": nrm((N_EVEN, d, d), d ** -0.5),
        "ev_gmlp_norm": gain((N_EVEN, GMLP_GROUPS, GMLP_GROUP_DIM)),
        "ev_gmlp_ws": nrm((N_EVEN, GMLP_GROUPS, GMLP_CHUNK, GMLP_CHUNK), 0.5 * GMLP_CHUNK ** -0.5),
        "ev_gmlp_b": gain((N_EVEN, GMLP_GROUPS, GMLP_CHUNK)),
        "ev_w_out": nrm((N_EVEN, MIX_OUT_WIDTH, D_MODEL), MIX_OUT_WIDTH ** -0.5),
        "od_norm": gain((N_ODD, D_MODEL)),
        "od_w_in": nrm((N_ODD, D_MODEL, 3 * SCONV_WIDTH), D_MODEL ** -0.5),
        "od_conv_w": nrm((N_ODD, CONV_WIDTH, SCONV_WIDTH), CONV_WIDTH ** -0.5),
        "od_w_out": nrm((N_ODD, SCONV_WIDTH, D_MODEL), SCONV_WIDTH ** -0.5),
        "ffn_norm": gain((DEPTH, D_MODEL)),
        "ffn_w_in": nrm((DEPTH, D_MODEL, 2 * D_FF), D_MODEL ** -0.5),
        "ffn_conv_w": nrm((DEPTH, CONV_WIDTH, D_FF), CONV_WIDTH ** -0.5),
        "ffn_conv_b": nrm((DEPTH, D_FF), 0.01),
        "ffn_w_down": nrm((DEPTH, D_FF, D_MODEL), D_FF ** -0.5),
    }

def reference(x, ev_norm, ev_w_in, ev_q_gain, ev_k_gain, ev_cmp_pe, ev_cmp_k_w1, ev_cmp_k_w2,
              ev_cmp_v_w1, ev_cmp_v_w2, ev_gmlp_norm, ev_gmlp_ws, ev_gmlp_b, ev_w_out,
              od_norm, od_w_in, od_conv_w, od_w_out,
              ffn_norm, ffn_w_in, ffn_conv_w, ffn_conv_b, ffn_w_down):
    for i in range(DEPTH):
        j = i // 2
        if i % 2 == 0:
            x = x + even_mixer(x, ev_norm[j], ev_w_in[j], ev_q_gain[j], ev_k_gain[j], ev_cmp_pe[j],
                               ev_cmp_k_w1[j], ev_cmp_k_w2[j], ev_cmp_v_w1[j], ev_cmp_v_w2[j],
                               ev_gmlp_norm[j], ev_gmlp_ws[j], ev_gmlp_b[j], ev_w_out[j])
        else:
            x = x + odd_mixer(x, od_norm[j], od_w_in[j], od_conv_w[j], od_w_out[j])
        x = x + conv_ffn(x, ffn_norm[i], ffn_w_in[i], ffn_conv_w[i], ffn_conv_b[i], ffn_w_down[i])
    return x


_drawn_inputs = setup_inputs


def setup_inputs(seed=0):
    import zlib

    import numpy as np

    out = dict(_drawn_inputs(seed))
    spreads = {}
    factors = {'ev_norm': 3.256,
     'ev_q_gain': 27.219,
     'ev_k_gain': 30.207,
     'ev_gmlp_norm': 44.834,
     'ev_gmlp_b': 15.785,
     'ffn_conv_b': 59.583,
     'ev_cmp_pe': 3.448,
     'od_norm': 8.0,
     'ffn_norm': 8.0}
    for name, (base, spread) in spreads.items():
        noise = np.random.default_rng([zlib.crc32(name.encode()), seed]).standard_normal(out[name].shape)
        drawn = base * np.exp(spread * noise) if base else spread * noise
        out[name] = __import__('jax').numpy.asarray(drawn.astype(out[name].dtype))
    for name, factor in factors.items():
        out[name] = (out[name] * factor).astype(out[name].dtype)
    return out
```

```python
from contextlib import ExitStack

import concourse.bass as bass
from concourse import mybir

F32 = mybir.dt.float32
F32R = mybir.dt.float32r
ACT = mybir.ActivationFunctionType
ALU = mybir.AluOpType
AX_X = mybir.AxisListType.X

P = 128
TOK = 256
D_MODEL = 2048
KT = D_MODEL // P
D_FF = 5632
FT = D_FF // P
HALF_FT = FT // 2
FF_SLAB_TILES = HALF_FT // 2
HEADS, KV, GROUP = 8, 2, 4
CMP_BLOCK, CMP_STRIDE = 32, 16
N_CMP = (TOK - CMP_BLOCK) // CMP_STRIDE + 1
CMP_PAD = 16
EPS = 1e-6
NEG = -1e30
SMALL = 1e-30

WIDE = KT * P
NARROW = FF_SLAB_TILES * P
AHEAD = 3
RING = 4
BANKS = 4


class Stage:

    def __init__(self, before, slabs, width, per_chunk, chunks=None):
        self.slab0 = before.slab0 + before.slabs if before else 0
        self.chunk0 = before.chunk0 + before.chunks if before else 0
        self.slabs, self.width, self.per_chunk = slabs, width, per_chunk
        self.chunks = slabs // per_chunk if chunks is None else chunks


def plan():
    s = {}
    s["kv"] = Stage(None, 13, WIDE, 1)
    s["compress"] = Stage(s["kv"], 4, WIDE, 2, chunks=0)
    s["heads"] = Stage(s["compress"], 3 * HEADS, WIDE, 1)
    s["mix_out"] = Stage(s["heads"], KT, WIDE, 1)
    before = s["mix_out"]
    for layer in range(2):
        if layer:
            s["conv_in"] = Stage(before, 3 * KT, WIDE, 1)
            s["conv_out"] = Stage(s["conv_in"], KT, WIDE, 1)
            before = s["conv_out"]
        for half in range(2):
            s["up", layer, half] = Stage(before, 2 * HALF_FT, WIDE, 1)
            s["down", layer, half] = Stage(s["up", layer, half], 2 * KT, NARROW, 2)
            before = s["down", layer, half]
    return s


STAGES = plan()
TOTAL = sum(st.slabs for st in STAGES.values())


def width_of(slab):
    for st in STAGES.values():
        if st.slab0 <= slab < st.slab0 + st.slabs:
            return st.width
    return None


class Turn:

    def __init__(self, i=None, k=0):
        self.i, self.k = i, k

    def at(self, base, step):
        return base + step * self.k if self.i is None else self.i * step + base


def wait(eng, sem, value):
    if not isinstance(value, int) or value > 0:
        eng.wait_ge(sem, value)


def build(nc, io):
    with ExitStack() as ctx:
        def sb(name, shape, dt=F32):
            return ctx.enter_context(nc.sbuf_tensor(name, shape, dt))

        def sem(name):
            return ctx.enter_context(nc.semaphore(name))

        raw = sb("raw", [P, RING, WIDE // 2])
        w_hi = sb("w_hi", [P, RING, WIDE], F32R)
        w_lo = sb("w_lo", [P, RING, WIDE], F32R)
        x = sb("x_res", [P, KT, TOK])
        xn = sb("xn", [P, KT, 2 * TOK], F32R)
        lo_part = sb("lo_part", [P, 2, TOK])
        sums = sb("sums", [P, TOK])
        gp = sb("gate_padded", [P, 2, TOK + 2])
        cva = sb("conv_a_buf", [P, TOK])
        cvb = sb("conv_b_buf", [P, TOK])
        cvc = sb("conv_c_buf", [P, 2, TOK])
        sil = sb("silu_buf", [P, 2, TOK])
        scaled = sb("scaled_buf", [P, TOK])
        prod = sb("prod_buf", [P, TOK])
        sq = sb("sq", [P, 2, TOK])
        ssq = sb("ssq", [P, TOK])
        rms = cvb
        rstd = sb("rstd", [P, TOK])
        ones = sb("ones", [P, P])
        ident = sb("ident", [P, P])
        gains = sb("gains", [P, 4, KT])
        ffn_cw = sb("ffn_cw", [P, 2, FT, 4])
        od_cw = sb("od_cw", [P, KT, 3])
        with nc.sbuf_tensor("hidden", [P, HALF_FT, 2 * TOK], F32R) as hidden:
            pass
        mix = sb("mix", [P, KT, 2 * TOK], F32R)
        with nc.sbuf_tensor("kvc", [P, 4, TOK], F32) as kvc:
            pass
        qn = sb("qn", [P, GROUP, TOK])
        kn = sb("kn", [P, 2, KV, TOK])
        vtok = sb("vtok", [P, KV, 5, P])
        with nc.sbuf_tensor("blk", [P, CMP_BLOCK, KV * N_CMP], F32) as blk:
            pass
        pt0 = sb("pt0", [P, 2, TOK])
        pt1 = sb("pt1", [P, 4, P])
        p0 = sb("p0", [P, 2, P])
        p1 = sil
        pc = sb("pc", [P, 2, CMP_PAD])
        pcp = sb("pcp", [P, 2, P])
        q_rms = sb("q_rms_buf", [P, GROUP, 2])
        q_r = sb("q_r_buf", [P, GROUP, 2])
        stat = sb("stat", [P, 4, 2, 3])
        gates = sb("gates", [P, 2, HEADS, 3])
        kcn = sb("kcn", [P, KV * CMP_PAD])
        hk = sb("hk", [P, KV, CMP_PAD])
        kct = sb("kct", [P, 3, KV * CMP_PAD])
        causal = sb("causal", [P, TOK])
        cmp_neg = sb("cmp_neg", [P, 2, CMP_PAD])
        cmp_keep = sb("cmp_keep", [P, 2, CMP_PAD])
        with nc.sbuf_tensor("w2", [P, 2, P], F32) as w2:
            w2k, w2v = w2[:, 0, :], w2[:, 1, :]
        vn = sb("vn", [P, 2, P])
        with nc.sbuf_tensor("hv", [P, KV, P], F32) as hv:
            pass
        v_act = sb("v_act", [P, TOK])
        pe_t = sb("pe_t", [P, CMP_BLOCK])
        q_gain = sb("q_gain", [P, 2])
        k_gain = sb("k_gain", [P, 3])
        g_gain = sb("g_gain", [P, HEADS])
        ws = sb("ws", [P, 2, P])
        g_bias = sb("g_bias", [P, 2, P])
        u_act = sb("u_act", [P, TOK])
        mv = sb("mv", [P, 2, 2])
        vstd = sb("vstd", [P, 3, 2])

        acc = [ctx.enter_context(nc.psum_tensor(f"acc{b}", [P, 512], F32)) for b in range(BANKS)]
        bank4, bank5, bank6, bank7 = (ctx.enter_context(nc.psum_tensor(f"bank{b}", [P, 512], F32)) for b in range(4, 8))

        raw_in = [sem(f"raw_in{i}") for i in range(RING)]
        names = """hi_made lo_made slab_used lo_copied chunk_summed
            x_loaded params_in x_updated x_squared x_rounded x_split ssq_added norm_summed rms_made rstd_made ssq_cleared
            consts_made pads_made
            gate_scaled conv_a conv_b conv_c silu_done up_scaled h_made h_rounded h_split
            c_scaled b_in_scaled cx_made b_scaled bc_made mix_rounded mix_split
            kv_scaled k_squared aux_made aux_read k_recip k_normed sig_done
            blk_made blk_rounded blk_split cmp_acc cmp_lo cmp_sum cmp_gelu kc_made kc_copied kc_squared kc_ms kc_rms kc_recip kc_normed vc_made vc_copied
            qg_made values_placed q_scaled q_squared q_ms_made q_rms_made q_recip q_gained scores_made masked maxed max_scaled exp_done cmp_masked cmp_summed
            sum_floored sum_recip weight_made probs_scaled turned turned_a turned_b head_made head_rounded
            v_scaled v_gelu v_turned v_summed v_mean v_centred v_squared v_std v_recip v_normed g_mixed u_scaled u_gelu g_biased g_prod
           
            ws_in ws_masked bias_in out_stored""".split()
        s = {n: sem(n) for n in names}

        block = ctx.enter_context(nc.Block())

        def ring(slab):
            return slab % RING

        def blk_hl(which):
            n = CMP_BLOCK * 2 * KV * N_CMP
            flat = mix[:, :, :].rearrange("p k t -> p (k t)")
            return flat[:, which * n:(which + 1) * n].rearrange("p (l c) -> p l c", l=CMP_BLOCK)

        def ahead_width(stage, turn, slab):
            return stage.width if turn.i is not None else width_of(slab)

        def turns(eng, stage, per_turn, body):
            n = stage.slabs // per_turn
            end = stage.slab0 + stage.slabs
            peel = width_of(end) != stage.width
            with eng.Fori(0, n - peel) as i:
                body(Turn(i))
            if peel:
                body(Turn(None, n - 1))

        def kn_chunk(t):
            i = K_CHUNKS.index(t)
            return kn[:, i // 2, i % 2, :]

        @block.sync
        def _(sp):
            def load_slab(stage, turn, j, src, step, src0):
                for half in range(2):
                    static = 2 * (stage.slab0 + j) + half
                    slot = static % RING
                    w = stage.width // 2
                    piece = turn.at(static - RING + 1, 2 * step)
                    wait(sp, s["lo_made"], piece)
                    sp.dma_start(raw[:, slot, 0:w], src(turn.at(src0 + j, step), half * w, w)).then_inc(raw_in[slot], 16)

            def load_stage(stage, src, src0=0):
                first = stage.slabs % 2 + (0 if stage.slab0 else RING // 2)
                for j in range(first):
                    load_slab(stage, Turn(), j, src, 2, src0)
                with sp.Fori(0, (stage.slabs - first) // 2) as i:
                    for j in range(2):
                        load_slab(stage, Turn(i), first + j, src, 2, src0)

            def stream(name):
                t = io[name]

                def src(n, lo, w):
                    if isinstance(n, int):
                        return t[n, :, lo:lo + w]
                    return t[bass.ds(n, 1), :, lo:lo + w].rearrange("a p w -> (a p) w")
                return src

            for quarter in range(4):
                k = KT // 4
                sp.dma_start(x[:, quarter * k:(quarter + 1) * k, :],
                             io["x"][quarter * k:(quarter + 1) * k].rearrange("k p t -> p k t")).then_inc(s["x_loaded"], 16)
            load_stage(STAGES["kv"], stream("mixer_in"))
            load_stage(STAGES["compress"], stream("cmp_w1"))
            load_stage(STAGES["heads"], stream("mixer_in"), STAGES["kv"].slabs)
            load_stage(STAGES["mix_out"], stream("mixer_out"))
            for layer in range(2):
                if layer:
                    load_stage(STAGES["conv_in"], stream("conv_in"))
                    load_stage(STAGES["conv_out"], stream("conv_out"))
                for half in range(2):
                    load_stage(STAGES["up", layer, half], stream("ffn_up"), (2 * layer + half) * 2 * HALF_FT)
                    load_stage(STAGES["down", layer, half], stream("ffn_down"), (2 * layer + half) * 2 * KT)
            done = 5 * KT
            for quarter in range(4):
                k = KT // 4
                sp.wait_ge(s["x_updated"], done + (quarter + 1) * k)
                sp.dma_start(io["out"][quarter * k:(quarter + 1) * k].rearrange("k p t -> p k t"),
                             x[:, quarter * k:(quarter + 1) * k, :]).then_inc(s["out_stored"], 16)
            sp.wait_ge(s["out_stored"], 64)

        @block.gpsimd
        def _(pool):
            n_par = 0
            for dst, name in ((gains[:, :, :], "gains"), (ffn_cw[:, :, :, :], "ffn_cw"), (od_cw[:, :, :], "od_cw"),
                              (w2k, "w2k"), (w2v, "w2v"), (pe_t[:, :], "pe"), (q_gain[:, 0:1], "q_gain"),
                              (k_gain[:, :], "k_gain"), (g_gain[:, :], "g_gain")):
                pool.dma_start(dst, io[name]).then_inc(s["params_in"], 16)
                n_par += 1
            assert n_par == N_PARAMS
            pool.memset(ones[:, :], 1.0).then_inc(s["consts_made"], 1)
            pool.memset(ident[:, :], 1.0).then_inc(s["consts_made"], 1)
            pool.memset(causal[:, :], 0.0).then_inc(s["consts_made"], 1)
            pool.memset(cmp_neg[:, :, :], 0.0).then_inc(s["consts_made"], 1)
            pool.memset(cmp_keep[:, :, :], 1.0).then_inc(s["consts_made"], 1)
            pool.wait_ge(s["consts_made"], 5)
            pool.affine_select(out=ident[:, :], in_=ident[:, :], pattern=[[-1, P]], compare_op=ALU.is_equal,
                               fill=0.0, base=0, channel_multiplier=1).then_inc(s["consts_made"], 1)
            pool.affine_select(out=causal[:, P:TOK], in_=causal[:, P:TOK], pattern=[[-1, P]], compare_op=ALU.is_ge,
                               fill=NEG, base=0, channel_multiplier=1).then_inc(s["consts_made"], 1)
            for half in range(2):
                for dst, fill in ((cmp_neg, NEG), (cmp_keep, 0.0)):
                    pool.affine_select(out=dst[:, half, :], in_=dst[:, half, :], pattern=[[-CMP_STRIDE, CMP_PAD]],
                                       compare_op=ALU.is_ge, fill=fill, base=half * P - (CMP_BLOCK - 1),
                                       channel_multiplier=1).then_inc(s["consts_made"], 1)
            for g in range(HEADS):
                b = g % 2
                wait(pool, s["g_biased"], g - 1)
                pool.dma_start(ws[:, b, :], io["ws"][g]).then_inc(s["ws_in"], 16)
                pool.wait_ge(s["ws_in"], 16 * (g + 1))
                pool.dma_start(g_bias[:, b, :], io["g_bias"][g:g + 1, :].broadcast_to([P, P])).then_inc(s["bias_in"], 16)
                pool.wait_ge(s["bias_in"], 16 * (g + 1))
                pool.affine_select(out=ws[:, b, :], in_=ws[:, b, :], pattern=[[1, P]], compare_op=ALU.is_ge,
                                   fill=0.0, base=0, channel_multiplier=-1).then_inc(s["ws_masked"], 1)

        @block.tensor
        def _(pe):
            def tile_products(bank, slot, tile, rhs_hl, n, first, last):
                hi = w_hi[:, slot, tile * P:(tile + 1) * P]
                lo = w_lo[:, slot, tile * P:(tile + 1) * P]
                if last:
                    pe.matmul(bank[:, 0:n], lo, rhs_hl[:, 0:n], start=False, stop=False)
                    return pe.matmul(bank[:, 0:2 * n], hi, rhs_hl, start=first, stop=True)
                pe.matmul(bank[:, 0:2 * n], hi, rhs_hl, start=first, stop=False)
                return pe.matmul(bank[:, 0:n], lo, rhs_hl[:, 0:n], start=False, stop=False)

            def chunk(stage, turn, step, j, rhs, tiles, ready=None):
                c = stage.chunk0 + j
                bank = acc[c % BANKS]
                wait(pe, s["chunk_summed"], turn.at(c - BANKS + 1, step))
                n = stage.per_chunk
                for part in range(n):
                    slab = stage.slab0 + n * j + part
                    pe.wait_ge(s["lo_made"], turn.at(2 * (slab + 1), 2 * n * step))
                    for t in range(tiles):
                        k = part * tiles + t
                        if ready:
                            ready(k)
                        mm = tile_products(bank, ring(slab), t, rhs(k), TOK, k == 0, k == n * tiles - 1)
                    mm.then_inc(s["slab_used"], 1)

            def when_x_split(norm):
                def ready(k):
                    if k == 0:
                        pe.wait_ge(s["x_split"], norm * KT + KT - 4)
                    if k >= KT - 4:
                        pe.wait_ge(s["x_split"], norm * KT + k + 1)
                return ready

            def sum_of_squares(norm):
                pe.wait_ge(s["ssq_added"], (norm + 1) * KT)
                if norm == 0:
                    pe.wait_ge(s["consts_made"], N_CONSTS)
                pe.matmul(bank4[:, 0:TOK], ones[:, :], ssq[:, :], start=True, stop=True).then_inc(s["norm_summed"], 1)

            def x_tile(k):
                return xn[:, k, :]

            def mix_tile(k):
                return mix[:, k, :]

            kv = STAGES["kv"]

            def kv_aux(t):
                bank = acc[t % BANKS]
                if t in K_CHUNKS:
                    pe.wait_ge(s["k_squared"], K_CHUNKS.index(t) + 1)
                    mm = pe.matmul(bank[:, 0:TOK], ones[:, :], sq[:, K_CHUNKS.index(t) % 2, :], start=True, stop=True)
                else:
                    if t in V_CHUNKS:
                        pe.wait_ge(s["kv_scaled"], t + 1)
                        src = cvc[:, V_CHUNKS.index(t) % 2, :]
                    else:
                        pe.wait_ge(s["sig_done"], 1)
                        src = scaled[:, :]
                    for half in range(2):
                        mm = pe.transpose(bank[:, half * P:(half + 1) * P], src[:, half * P:(half + 1) * P], ident[:, :])
                mm.then_inc(s["aux_made"], 1)

            for t in range(kv.slabs):
                if t >= 8:
                    pe.wait_ge(s["aux_read"], t - BANKS - 4 + 1)
                chunk(kv, Turn(), 1, t, x_tile, KT, when_x_split(0) if t == 0 else None)
                if t == 0:
                    sum_of_squares(0)
                if t - 1 in K_CHUNKS + V_CHUNKS:
                    kv_aux(t - 1)

            cp = STAGES["compress"]
            for which in range(2):
                bank = (bank4, bank5)[which]
                if which == 0:
                    pe.wait_ge(s["rms_made"], 1)
                pe.wait_ge(s["blk_split"], which + 1)
                for part in range(2):
                    slab = cp.slab0 + 2 * which + part
                    pe.wait_ge(s["lo_made"], 2 * (slab + 1))
                    for t in range(KT):
                        pos = part * KT + t
                        mm = tile_products(bank, ring(slab), t, blk_hl(which)[:, pos, :], KV * N_CMP, pos == 0,
                                           pos == CMP_BLOCK - 1)
                    mm.then_inc(s["slab_used"], 1)
                    if which == 0 and part == 0:
                        kv_aux(GATE_CHUNK)
                if which == 0:
                    continue
                pe.wait_ge(s["cmp_gelu"], 1)
                pe.matmul(bank6[:, 0:KV * CMP_PAD], w2k, hk[:, :, :].rearrange("p g n -> p (g n)"),
                          start=True, stop=True).then_inc(s["kc_made"], 1)
                pe.wait_ge(s["kc_squared"], 1)
                pe.matmul(bank6[:, 0:KV * CMP_PAD], ones[:, :], kct[:, 1, :], start=True, stop=True).then_inc(s["kc_ms"], 1)
                pe.wait_ge(s["cmp_gelu"], 2)
                for g in range(KV):
                    mm = pe.matmul(bank7[:, g * P:(g + 1) * P], hv[:, g, :], w2v, start=True, stop=True)
                mm.then_inc(s["vc_made"], 1)
            pe.wait_ge(s["aux_read"], 9)

            hd = STAGES["heads"]

            def heads_turn(turn):
                def head(j):
                    return turn.at(j + 1, GROUP)

                def bank_of(t):
                    return acc[(hd.chunk0 + t) % BANKS]

                def mean_square(j):
                    pe.wait_ge(s["q_squared"], head(j))
                    for half in range(2):
                        mm = pe.matmul(bank_of(j)[:, half:half + 1], sq[:, j % 2, half * P:(half + 1) * P], ones[:, 0:1],
                                       start=True, stop=True)
                    mm.then_inc(s["q_ms_made"], 1)

                def scores(j):
                    pe.wait_ge(s["q_gained"], head(j))
                    if j == 0:
                        pe.wait_ge(s["k_normed"], 4)
                        pe.wait_ge(s["kc_normed"], 1)
                    k = [kn[:, b, bass.ds(turn.at(0, 1), 1), :].rearrange("p a t -> p (a t)") for b in range(2)]
                    kc = kcn[:, bass.ds(turn.at(0, CMP_PAD), CMP_PAD)]
                    for half in range(2):
                        q = qn[:, j, half * P:(half + 1) * P]
                        pe.matmul(bank5[:, 256 + half * CMP_PAD:256 + (half + 1) * CMP_PAD], q, kc, start=True, stop=True)
                        for b in range(2):
                            if half == 0:
                                mm = pe.matmul(bank5[:, b * P:(b + 1) * P], q, k[b][:, 0:P], start=True, stop=True)
                            else:
                                mm = pe.matmul(bank6[:, b * TOK:(b + 1) * TOK], q, k[b], start=True, stop=True)
                    mm.then_inc(s["scores_made"], 1)

                def turn_probs(j):
                    pe.wait_ge(s["probs_scaled"], head(j))
                    if j:
                        pe.wait_ge(s["head_rounded"], turn.at(2 * j, 2 * GROUP))
                    for b in range(2):
                        pe.transpose(bank7[:, b * TOK:b * TOK + P], p0[:, b, :], ident[:, :])
                        pe.transpose(bank7[:, b * TOK + P:(b + 1) * TOK], p1[:, b, 0:P], ident[:, :])
                        pe.transpose(bank4[:, b * P:(b + 1) * P], p1[:, b, P:TOK], ident[:, :])
                        mm = pe.transpose(bank4[:, (2 + b) * P:(3 + b) * P], pcp[:, b, :], ident[:, :])
                    mm.then_inc(s["turned"], 1)

                def head_out(j):
                    pe.wait_ge(s["turned_a"], head(j))
                    pe.wait_ge(s["turned_b"], head(j))
                    if j == 0:
                        pe.wait_ge(s["values_placed"], turn.at(1, 1))
                    pe.matmul(bank7[:, 0:TOK], vtok[:, 0, 0, :], pt1[:, 2:4, :].rearrange("p a t -> p (a t)"), start=True, stop=False)
                    for b in range(2):
                        pe.matmul(bank7[:, P:TOK], vtok[:, 0, 2 + 2 * b, :], pt1[:, b, :], start=False, stop=False)
                    for b in range(2):
                        mm = pe.matmul(bank7[:, 0:TOK], vtok[:, 0, 1 + 2 * b, :], pt0[:, b, :], start=False, stop=b == 1)
                    mm.then_inc(s["head_made"], 1)

                def turn_values(j):
                    pe.wait_ge(s["v_gelu"], head(j))
                    bank = bank_of(GROUP + 2 * j)
                    for half in range(2):
                        mm = pe.transpose(bank[:, half * P:(half + 1) * P], v_act[:, half * P:(half + 1) * P], ident[:, :])
                    mm.then_inc(s["v_turned"], 1)

                def mix_tokens(j):
                    pe.wait_ge(s["v_normed"], head(j))
                    pe.wait_ge(s["ws_masked"], head(j))
                    bank = bank_of(GROUP + 2 * j)
                    for half in range(2):
                        mm = pe.matmul(bank[:, half * P:(half + 1) * P], vn[:, half, :], ws[:, j % 2, :], start=True, stop=True)
                    mm.then_inc(s["g_mixed"], 1)

                todo = {1: [(mean_square, 0)], 2: [(scores, 0), (mean_square, 1)], 3: [(mean_square, 2)],
                        4: [(mean_square, 3), (turn_probs, 0), (scores, 1)], 5: [(head_out, 0), (turn_values, 0)],
                        6: [(mix_tokens, 0), (turn_probs, 1), (scores, 2)], 7: [(head_out, 1), (turn_values, 1)],
                        8: [(mix_tokens, 1), (turn_probs, 2), (scores, 3)], 9: [(head_out, 2), (turn_values, 2)],
                        10: [(mix_tokens, 2), (turn_probs, 3)], 11: [(head_out, 3), (turn_values, 3), (mix_tokens, 3)]}
                for t in range(3 * GROUP):
                    if GROUP <= t < 2 * GROUP:
                        pe.wait_ge(s["q_rms_made"], head(t - GROUP))
                    if t in (8, 10):
                        pe.wait_ge(s["g_biased"], head(t // 2 - 4))
                    chunk(hd, turn, 3 * GROUP, t, x_tile, KT)
                    for step, j in todo.get(t, []):
                        step(j)
                pe.wait_ge(s["head_rounded"], turn.at(2 * GROUP, 2 * GROUP))
                pe.wait_ge(s["g_biased"], head(3))

            with pe.Fori(0, KV) as g:
                heads_turn(Turn(g))

            def out_projection(stage, split):
                def ready(k):
                    if k == 0:
                        pe.wait_ge(s["mix_split"], split)
                for j in range(BANKS):
                    chunk(stage, Turn(), BANKS, j, mix_tile, KT, ready if j == 0 else None)
                with pe.Fori(1, KT // BANKS) as i:
                    for j in range(BANKS):
                        chunk(stage, Turn(i), BANKS, j, mix_tile, KT)

            out_projection(STAGES["mix_out"], HEADS)

            for layer in range(2):
                if layer:
                    st = STAGES["conv_in"]
                    for j in range(12):
                        chunk(st, Turn(), 12, j, x_tile, KT, when_x_split(2) if j == 0 else None)
                        if j == 0:
                            sum_of_squares(2)
                    with pe.Fori(1, st.chunks // 12) as i:
                        for j in range(12):
                            chunk(st, Turn(i), 12, j, x_tile, KT)
                    out_projection(STAGES["conv_out"], HEADS + KT)
                for half in range(2):
                    st = STAGES["up", layer, half]
                    if half == 0:
                        for j in range(BANKS):
                            chunk(st, Turn(), BANKS, j, x_tile, KT, when_x_split(1 + 2 * layer) if j == 0 else None)
                            if j == 0:
                                sum_of_squares(1 + 2 * layer)
                    with pe.Fori(1 - half, st.chunks // BANKS) as i:
                        for j in range(BANKS):
                            chunk(st, Turn(i), BANKS, j, x_tile, KT)
                    st = STAGES["down", layer, half]
                    base = (2 * layer + half) * HALF_FT

                    def ready(k):
                        if k == 0:
                            pe.wait_ge(s["h_split"], base + HALF_FT - 4)
                        if k >= HALF_FT - 4:
                            pe.wait_ge(s["h_split"], base + k + 1)
                    for j in range(BANKS):
                        chunk(st, Turn(), BANKS, j, lambda k: hidden[:, k, :], FF_SLAB_TILES, ready if j == 0 else None)
                    with pe.Fori(1, st.chunks // BANKS) as i:
                        for j in range(BANKS):
                            chunk(st, Turn(i), BANKS, j, lambda k: hidden[:, k, :], FF_SLAB_TILES)

        @block.scalar
        def _(act):
            def round_slab(stage, turn, j, step):
                static = stage.slab0 + j + AHEAD
                slab = turn.at(static, step)
                w = ahead_width(stage, turn, slab)
                if w is None:
                    return
                round_at(turn, static, step, w)

            def round_at(turn, static, step, w):
                h = w // 2
                wait(act, s["slab_used"], turn.at(static - RING + 1, step))
                for half in range(2):
                    piece = 2 * static + half
                    slot = piece % RING
                    act.wait_ge(raw_in[slot], turn.at(16 * (piece // RING + 1), 16 * step // 2))
                    act.activation(w_hi[:, ring(static), half * h:(half + 1) * h], raw[:, slot, 0:h], ACT.Copy).then_inc(s["hi_made"], 1)

            def copy_lo(stage, turn, j, step, per_turn=None):
                c = stage.chunk0 + j
                n = stage.per_chunk
                per = n * step
                act.wait_ge(s["slab_used"], turn.at(stage.slab0 + n * (j + 1), per))
                wait(act, s["chunk_summed"], turn.at(c - 1, step))
                act.activation(lo_part[:, c % 2, :], acc[c % BANKS][:, TOK:2 * TOK], ACT.Copy).then_inc(s["lo_copied"], 1)

            def square_x(first, turn, j, step, updated):
                if updated is not None:
                    act.wait_ge(s["x_updated"], turn.at(updated + j + 1, step))
                wait(act, s["ssq_added"], turn.at(first + j - 1, step))
                tile = turn.at(j, step)
                src = x[:, tile, :] if isinstance(tile, int) else x[:, bass.ds(tile, 1), :].rearrange("p a t -> p (a t)")
                act.activation(sq[:, j % 2, :], src, ACT.Square).then_inc(s["x_squared"], 1)

            def root_mean(norm):
                act.wait_ge(s["norm_summed"], norm + 1)
                act.activation(rms[:, :], bank4[:, 0:TOK], ACT.Sqrt, bias=eps[:, :], scale=1.0 / D_MODEL).then_inc(s["rms_made"], 1)

            eps = stat[:, 3, 0, 0:1]
            for a in range(AHEAD):
                round_at(Turn(), a, 1, WIDE)
            act.wait_ge(s["pads_made"], N_PADS)
            act.wait_ge(s["x_loaded"], 64)
            for n in range(KT):
                square_x(0, Turn(), n, 1, None)

            kv = STAGES["kv"]

            def read_aux(t):
                act.wait_ge(s["aux_made"], t - 3)
                bank = acc[t % BANKS]
                if t in K_CHUNKS:
                    i = K_CHUNKS.index(t)
                    wait(act, s["k_recip"], i)
                    act.activation(sil[:, 0, :], bank[:, 0:TOK], ACT.Sqrt, bias=eps[:, :], scale=1.0 / P).then_inc(s["aux_read"], 1)
                elif t in V_CHUNKS:
                    i = V_CHUNKS.index(t)
                    b, g = i // 2, i % 2
                    act.activation(vtok[:, g, 1 + 2 * b:3 + 2 * b, :].rearrange("p a t -> p (a t)"), bank[:, 0:TOK],
                                   ACT.Copy).then_inc(s["aux_read"], 1)
                else:
                    act.activation(gates[:, :, :, :].rearrange("p a h b -> p a (h b)"),
                                   bank[:, 0:TOK].rearrange("p (a c) -> p a c", a=2)[:, :, 0:3 * HEADS],
                                   ACT.Copy).then_inc(s["aux_read"], 1)

            for t in range(kv.slabs):
                round_slab(kv, Turn(), t, 1)
                if t == 0:
                    root_mean(0)
                copy_lo(kv, Turn(), t, 1)
                if t - 1 in K_CHUNKS + V_CHUNKS:
                    read_aux(t - 1)
                if t in K_CHUNKS:
                    act.wait_ge(s["kv_scaled"], t + 1)
                    wait(act, s["aux_made"], t - 4 if K_CHUNKS.index(t) >= 2 else 0)
                    act.activation(sq[:, K_CHUNKS.index(t) % 2, :], kn_chunk(t), ACT.Square).then_inc(s["k_squared"], 1)
                if t == GATE_CHUNK:
                    act.wait_ge(s["kv_scaled"], t + 1)
                    act.activation(scaled[:, :], prod[:, :], ACT.Sigmoid).then_inc(s["sig_done"], 1)

            cp = STAGES["compress"]
            for t in range(cp.slabs):
                round_slab(cp, Turn(), t, 1)
                if t == 0:
                    read_aux(GATE_CHUNK)
                if t % 2:
                    which = t // 2
                    act.wait_ge(s["slab_used"], cp.slab0 + t + 1)
                    n = KV * N_CMP
                    wait(act, s["cmp_sum"], which)
                    act.activation(prod[:, 0:n], (bank4, bank5)[which][:, n:2 * n], ACT.Copy).then_inc(s["cmp_lo"], 1)
                    act.wait_ge(s["cmp_sum"], which + 1)
                    dst = (hk, hv)[which][:, :, 0:N_CMP]
                    act.activation(dst, sums[:, 0:n].rearrange("p (g n) -> p g n", g=KV), ACT.Gelu_apprx_tanh).then_inc(s["cmp_gelu"], 1)
            act.wait_ge(s["kc_copied"], 1)
            act.activation(kct[:, 1, :], kct[:, 0, :], ACT.Square).then_inc(s["kc_squared"], 1)
            act.wait_ge(s["kc_ms"], 1)
            act.activation(kct[:, 2, :], bank6[:, 0:KV * CMP_PAD], ACT.Sqrt, bias=eps[:, :], scale=1.0 / P).then_inc(s["kc_rms"], 1)
            act.wait_ge(s["vc_made"], 1)
            act.activation(vtok[:, :, 0, :], bank7[:, 0:KV * P].rearrange("p (g f) -> p g f", g=KV), ACT.Copy).then_inc(s["vc_copied"], 1)

            hd = STAGES["heads"]

            def heads_turn(turn):
                def head(j):
                    return turn.at(j + 1, GROUP)

                def bank_of(t):
                    return acc[(hd.chunk0 + t) % BANKS]

                def q_root(j):
                    act.wait_ge(s["q_ms_made"], head(j))
                    act.activation(q_rms[:, j, :], bank_of(j)[:, 0:2], ACT.Sqrt, bias=eps[:, :], scale=1.0 / P).then_inc(s["q_rms_made"], 1)

                def exponentials(j):
                    act.wait_ge(s["max_scaled"], head(j))
                    for half in range(2):
                        act.activation(pc[:, half, :], pc[:, half, :], ACT.Exp, bias=stat[:, 1, half, 0:1],
                                       scale=q_r[:, j, half:half + 1])
                        for b in range(2):
                            src = (p0, p1)[half][:, b, :]
                            e = act.activation(src, src, ACT.Exp, bias=stat[:, 1, half, 1 + b:2 + b],
                                               scale=q_r[:, j, half:half + 1], accum_out=stat[:, 2, half, 1 + b:2 + b])
                    e.then_inc(s["exp_done"], 1)

                def copy_turned(j):
                    act.wait_ge(s["turned"], head(j))
                    act.activation(pt0[:, :, :].rearrange("p b t -> p (b t)"), bank7[:, :], ACT.Copy).then_inc(s["turned_a"], 1)

                def v_root(j):
                    act.wait_ge(s["v_centred"], head(j))
                    for half in range(2):
                        e = act.activation(v_act[:, half * P:(half + 1) * P], vn[:, half, :], ACT.Square,
                                           accum_out=vstd[:, 2, half:half + 1])
                    e.then_inc(s["v_squared"], 1)
                    act.wait_ge(s["v_squared"], head(j))
                    act.activation(vstd[:, 0, :], vstd[:, 2, :], ACT.Sqrt, bias=eps[:, :], scale=1.0 / P).then_inc(s["v_std"], 1)

                todo = {1: [(q_root, 0)], 2: [(exponentials, 0), (q_root, 1)], 3: [(q_root, 2)],
                        4: [(q_root, 3), (copy_turned, 0), (exponentials, 1)], 5: [(v_root, 0)],
                        6: [(copy_turned, 1), (exponentials, 2)], 7: [(v_root, 1)],
                        8: [(copy_turned, 2), (exponentials, 3)], 9: [(v_root, 2)],
                        10: [(copy_turned, 3)], 11: [(v_root, 3)]}
                for t in range(3 * GROUP):
                    round_slab(hd, turn, t, 3 * GROUP)
                    copy_lo(hd, turn, t, 3 * GROUP)
                    if t < GROUP:
                        act.wait_ge(s["q_scaled"], head(t))
                        if t >= 2:
                            act.wait_ge(s["q_ms_made"], head(t - 2))
                        act.activation(sq[:, t % 2, :], cvc[:, t % 2, :], ACT.Square).then_inc(s["q_squared"], 1)
                    elif t % 2 == 0:
                        j = (t - GROUP) // 2
                        act.wait_ge(s["v_scaled"], head(j))
                        act.activation(v_act[:, :], scaled[:, :], ACT.Gelu_apprx_tanh).then_inc(s["v_gelu"], 1)
                    else:
                        j = (t - GROUP) // 2
                        act.wait_ge(s["u_scaled"], head(j))
                        act.activation(u_act[:, :], prod[:, :], ACT.Gelu_apprx_tanh).then_inc(s["u_gelu"], 1)
                    for step, j in todo.get(t, []):
                        step(j)

            with act.Fori(0, KV) as g:
                heads_turn(Turn(g))

            def out_projection(stage, norm, updated):
                def body(turn):
                    for j in range(BANKS):
                        for p in range(stage.per_chunk):
                            round_slab(stage, turn, stage.per_chunk * j + p, stage.per_chunk * BANKS)
                        copy_lo(stage, turn, j, BANKS)
                        if norm is not None:
                            square_x(norm * KT, turn, j, BANKS, updated)
                turns(act, stage, BANKS * stage.per_chunk, body)

            out_projection(STAGES["mix_out"], 1, 0)
            for layer in range(2):
                if layer:
                    root_mean(2)
                    st = STAGES["conv_in"]

                    def body(turn):
                        for j in range(12):
                            round_slab(st, turn, j, 12)
                            copy_lo(st, turn, j, 12)
                    turns(act, st, 12, body)
                    out_projection(STAGES["conv_out"], 3, 3 * KT)
                root_mean(1 + 2 * layer)
                for half in range(2):
                    st = STAGES["up", layer, half]
                    pair0 = (2 * layer + half) * HALF_FT
                    tile0 = half * HALF_FT

                    def body(turn):
                        for j in range(4):
                            round_slab(st, turn, j, 4)
                            copy_lo(st, turn, j, 4)
                            if j % 2:
                                act.wait_ge(s["conv_c"], turn.at(pair0 + KT * layer + j // 2 + 1, 2))
                                f = turn.at(tile0 + j // 2, 2)
                                bias = ffn_cw[:, layer, f, 3:4] if isinstance(f, int) else \
                                    ffn_cw[:, layer, bass.ds(f, 1), 3:4].rearrange("p a b -> p (a b)")
                                act.activation(sil[:, j // 2, :], cvc[:, j // 2, :], ACT.Silu, bias=bias).then_inc(s["silu_done"], 1)
                    turns(act, st, 4, body)
                    out_projection(STAGES["down", layer, half], 2 if half == 1 and layer == 0 else None,
                                   (1 if layer == 0 else 4) * KT + half * KT)

        @block.vector
        def _(dve):
            def subtract_slab(stage, turn, j, step):
                static = stage.slab0 + j + AHEAD
                w = ahead_width(stage, turn, turn.at(static, step))
                if w is not None:
                    subtract_at(turn, static, step, w)

            def subtract_at(turn, static, step, w):
                h = w // 2
                for half in range(2):
                    piece = 2 * static + half
                    dve.wait_ge(s["hi_made"], turn.at(piece + 1, 2 * step))
                    part = slice(half * h, (half + 1) * h)
                    dve.tensor_tensor(w_lo[:, ring(static), part], raw[:, piece % RING, 0:h],
                                      w_hi[:, ring(static), part].bitcast(F32), ALU.subtract).then_inc(s["lo_made"], 1)
                if half:
                    dve.wait_ge(s["lo_made"], turn.at(2 * static + 1, 2 * step))

            def sum_chunk(stage, turn, j, step):
                c = stage.chunk0 + j
                dve.wait_ge(s["lo_copied"], turn.at(c + 1, step))
                dve.tensor_tensor(sums[:, :], acc[c % BANKS][:, 0:TOK], lo_part[:, c % 2, :], ALU.add).then_inc(s["chunk_summed"], 1)
                dve.wait_ge(s["chunk_summed"], turn.at(c + 1, step))
                return sums[:, :]

            def tile_of(t, tile):
                return t[:, tile, :] if isinstance(tile, int) else t[:, bass.ds(tile, 1), :].rearrange("p a t -> p (a t)")

            def split_x(norm, turn, j, step):
                first = norm * KT + j
                tile = turn.at(j, step)
                gain = tile_of(gains[:, norm, :].rearrange("p (k a) -> p k a", a=1), tile)
                hl = tile_of(xn, tile)
                dve.tensor_scalar(hl[:, 0:TOK], tile_of(x, tile), gain, None, ALU.mult).then_inc(s["x_rounded"], 1)
                dve.wait_ge(s["x_rounded"], turn.at(first + 1, step))
                dve.scalar_tensor_tensor(hl[:, TOK:2 * TOK], tile_of(x, tile), gain, hl[:, 0:TOK].bitcast(F32),
                                         ALU.mult, ALU.subtract).then_inc(s["x_split"], 1)
                dve.wait_ge(s["x_squared"], turn.at(first + 1, step))
                wait(dve, s["ssq_added"], turn.at(first, step))
                dve.tensor_tensor(ssq[:, :], ssq[:, :], sq[:, j % 2, :], ALU.add).then_inc(s["ssq_added"], 1)

            def inverse_rms(norm):
                dve.wait_ge(s["rms_made"], norm + 1)
                dve.reciprocal(rstd[:, :], rms[:, :]).then_inc(s["rstd_made"], 1)
                dve.memset(ssq[:, :], 0.0).then_inc(s["ssq_cleared"], 1)
                dve.wait_ge(s["rstd_made"], norm + 1)
                dve.wait_ge(s["ssq_cleared"], norm + 1)

            def conv3(src, weight, dst, done):
                dve.tensor_scalar(cva[:, :], src[:, 2:TOK + 2], weight(2), None, ALU.mult).then_inc(s["conv_a"], 1)
                dve.wait_ge(s["conv_a"], done)
                dve.scalar_tensor_tensor(cvb[:, :], src[:, 1:TOK + 1], weight(1), cva[:, :], ALU.mult, ALU.add).then_inc(s["conv_b"], 1)
                dve.wait_ge(s["conv_b"], done)
                dve.scalar_tensor_tensor(dst, src[:, 0:TOK], weight(0), cvb[:, :], ALU.mult, ALU.add).then_inc(s["conv_c"], 1)

            dve.memset(gp[:, :, 0:2], 0.0).then_inc(s["pads_made"], 1)
            dve.memset(ssq[:, :], 0.0).then_inc(s["pads_made"], 1)
            dve.memset(hk[:, :, :], 0.0).then_inc(s["pads_made"], 1)
            dve.memset(hv[:, :, :], 0.0).then_inc(s["pads_made"], 1)
            dve.memset(pcp[:, :, :], 0.0).then_inc(s["pads_made"], 1)
            dve.memset(stat[:, 3, :, :], EPS).then_inc(s["pads_made"], 1)
            dve.wait_ge(s["pads_made"], N_PADS)
            for a in range(AHEAD):
                subtract_at(Turn(), a, 1, WIDE)
            dve.wait_ge(s["x_loaded"], 64)
            dve.wait_ge(s["params_in"], 16 * N_PARAMS)
            dve.wait_ge(s["consts_made"], N_CONSTS)
            dve.tensor_scalar(q_gain[:, 1:2], q_gain[:, 0:1], float(P) ** -0.5, None, ALU.mult).then_inc(s["qg_made"], 1)
            for n in range(KT):
                split_x(0, Turn(), n, 1)

            kv = STAGES["kv"]

            def after_aux(t):
                if t in K_CHUNKS:
                    i = K_CHUNKS.index(t)
                    dve.wait_ge(s["aux_read"], t - 3)
                    dve.reciprocal(sil[:, 1, :], sil[:, 0, :]).then_inc(s["k_recip"], 1)
                    dve.wait_ge(s["k_recip"], i + 1)
                    b = i // 2
                    dve.scalar_tensor_tensor(kn_chunk(t), kn_chunk(t), k_gain[:, 1 + b:2 + b], sil[:, 1, :],
                                             ALU.mult, ALU.mult).then_inc(s["k_normed"], 1)

            def make_blocks(which):
                src = kvc[:, 2 * which:2 * which + 2, :].rearrange("p g (m b) -> p b g m", b=CMP_STRIDE)
                n = KV * N_CMP
                for a in range(2):
                    dst = blk[:, a * CMP_STRIDE:(a + 1) * CMP_STRIDE, :].rearrange("p l (g n) -> p l g n", g=KV)
                    pos = pe_t[:, a * CMP_STRIDE:(a + 1) * CMP_STRIDE].unsqueeze(2).unsqueeze(3)
                    dve.tensor_tensor(dst, src[:, :, :, a:a + N_CMP], pos.broadcast_to([P, CMP_STRIDE, KV, N_CMP]),
                                      ALU.add).then_inc(s["blk_made"], 1)
                dve.wait_ge(s["blk_made"], 2 * (which + 1))
                dve.tensor_copy(blk_hl(which)[:, :, 0:n], blk[:, :, :]).then_inc(s["blk_rounded"], 1)
                dve.wait_ge(s["blk_rounded"], which + 1)
                dve.tensor_tensor(blk_hl(which)[:, :, n:2 * n], blk[:, :, :], blk_hl(which)[:, :, 0:n].bitcast(F32),
                                  ALU.subtract).then_inc(s["blk_split"], 1)

            for t in range(kv.slabs):
                subtract_slab(kv, Turn(), t, 1)
                if t == 0:
                    inverse_rms(0)
                total = sum_chunk(kv, Turn(), t, 1)
                if t < 4:
                    dst = kvc[:, t, :]
                elif t in K_CHUNKS:
                    dst = kn_chunk(t)
                elif t in V_CHUNKS:
                    dst = cvc[:, V_CHUNKS.index(t) % 2, :]
                else:
                    dst = prod[:, :]
                if t in V_CHUNKS and V_CHUNKS.index(t) >= 2:
                    dve.wait_ge(s["aux_made"], V_CHUNKS[V_CHUNKS.index(t) - 2] - 3)
                dve.tensor_tensor(dst, total, rstd[:, :], ALU.mult).then_inc(s["kv_scaled"], 1)
                if t in (1, 3):
                    dve.wait_ge(s["kv_scaled"], t + 1)
                    make_blocks(t // 2)
                if t - 1 in K_CHUNKS:
                    after_aux(t - 1)

            cp = STAGES["compress"]
            for t in range(cp.slabs):
                subtract_slab(cp, Turn(), t, 1)
                if t % 2:
                    which = t // 2
                    n = KV * N_CMP
                    dve.wait_ge(s["cmp_lo"], which + 1)
                    wait(dve, s["cmp_gelu"], which)
                    dve.tensor_tensor(sums[:, 0:n], (bank4, bank5)[which][:, 0:n], prod[:, 0:n], ALU.add).then_inc(s["cmp_sum"], 1)
            dve.wait_ge(s["kc_made"], 1)
            dve.tensor_copy(kct[:, 0, :], bank6[:, 0:KV * CMP_PAD]).then_inc(s["kc_copied"], 1)
            dve.wait_ge(s["kc_rms"], 1)
            dve.reciprocal(kcn[:, :], kct[:, 2, :]).then_inc(s["kc_recip"], 1)
            dve.wait_ge(s["kc_recip"], 1)
            dve.scalar_tensor_tensor(kcn[:, :], kct[:, 0, :], k_gain[:, 0:1], kcn[:, :], ALU.mult, ALU.mult).then_inc(s["kc_normed"], 1)
            dve.wait_ge(s["vc_copied"], 1)
            dve.wait_ge(s["aux_read"], 9)

            hd = STAGES["heads"]

            def split_mix(src, tile, count):
                hl = tile_of(mix, tile)
                dve.tensor_copy(hl[:, 0:TOK], src).then_inc(s["mix_rounded"], 1)
                dve.wait_ge(s["mix_rounded"], count)
                return dve.tensor_tensor(hl[:, TOK:2 * TOK], src, hl[:, 0:TOK].bitcast(F32), ALU.subtract)

            def heads_turn(turn):
                def head(j):
                    return turn.at(j + 1, GROUP)

                def bank_of(t):
                    return acc[(hd.chunk0 + t) % BANKS]

                def q_inverse(j):
                    dve.wait_ge(s["q_rms_made"], head(j))
                    dve.reciprocal(q_r[:, j, :], q_rms[:, j, :]).then_inc(s["q_recip"], 1)

                def softmax(j):
                    dve.wait_ge(s["scores_made"], head(j))
                    dve.wait_ge(s["q_recip"], head(j))
                    dve.tensor_tensor(p0[:, :, :], bank5[:, 0:2 * P].rearrange("p (b t) -> p b t", b=2),
                                      causal[:, P:TOK].unsqueeze(1).broadcast_to([P, 2, P]), ALU.add).then_inc(s["masked"], 1)
                    dve.tensor_tensor(p1[:, :, :], bank6[:, :].rearrange("p (b t) -> p b t", b=2),
                                      causal[:, :].unsqueeze(1).broadcast_to([P, 2, TOK]), ALU.add).then_inc(s["masked"], 1)
                    dve.tensor_tensor(pc[:, :, :], bank5[:, 2 * P:2 * P + 2 * CMP_PAD].rearrange("p (b t) -> p b t", b=2),
                                      cmp_neg[:, :, :], ALU.add).then_inc(s["masked"], 1)
                    dve.wait_ge(s["masked"], turn.at(3 * (j + 1), 3 * GROUP))
                    dve.tensor_reduce(stat[:, 0, 0, 1:3], p0[:, :, :], AX_X, ALU.max, negate=True).then_inc(s["maxed"], 1)
                    dve.tensor_reduce(stat[:, 0, 1, 1:3], p1[:, :, :], AX_X, ALU.max, negate=True).then_inc(s["maxed"], 1)
                    dve.tensor_reduce(stat[:, 0, :, 0:1].rearrange("p a b -> p (a b)"), pc[:, :, :], AX_X, ALU.max, negate=True).then_inc(s["maxed"], 1)
                    dve.wait_ge(s["maxed"], turn.at(3 * (j + 1), 3 * GROUP))
                    dve.scalar_tensor_tensor(stat[:, 1, :, :], stat[:, 0, :, :], -NEG / 10, q_r[:, j, :].unsqueeze(2).broadcast_to([P, 2, 3]),
                                             ALU.min, ALU.mult).then_inc(s["max_scaled"], 1)
                    dve.wait_ge(s["exp_done"], head(j))
                    dve.tensor_tensor(pc[:, :, :], pc[:, :, :], cmp_keep[:, :, :], ALU.mult).then_inc(s["cmp_masked"], 1)
                    dve.wait_ge(s["cmp_masked"], head(j))
                    dve.tensor_reduce(stat[:, 2, :, 0:1].rearrange("p a b -> p (a b)"), pc[:, :, :], AX_X, ALU.add).then_inc(s["cmp_summed"], 1)
                    dve.wait_ge(s["cmp_summed"], head(j))
                    dve.tensor_scalar(stat[:, 0, :, :], stat[:, 2, :, :], SMALL, None, ALU.max).then_inc(s["sum_floored"], 1)
                    dve.wait_ge(s["sum_floored"], head(j))
                    dve.reciprocal(stat[:, 1, :, :], stat[:, 0, :, :]).then_inc(s["sum_recip"], 1)
                    dve.wait_ge(s["sum_recip"], head(j))
                    gate = gates[:, :, bass.ds(turn.at(j, GROUP), 1), :].rearrange("p a h b -> p a (h b)")
                    dve.tensor_tensor(stat[:, 0, :, :], stat[:, 1, :, :], gate, ALU.mult).then_inc(s["weight_made"], 1)
                    dve.wait_ge(s["weight_made"], head(j))
                    for half in range(2):
                        dve.tensor_scalar(pcp[:, half, 0:CMP_PAD], pc[:, half, :], stat[:, 0, half, 0:1], None, ALU.mult)
                        for b in range(2):
                            src = (p0, p1)[half][:, b, :]
                            e = dve.tensor_scalar(src, src, stat[:, 0, half, 1 + b:2 + b], None, ALU.mult)
                    e.then_inc(s["probs_scaled"], 1)

                def copy_turned(j):
                    dve.wait_ge(s["turned"], head(j))
                    dve.tensor_copy(pt1[:, :, :].rearrange("p b t -> p (b t)"), bank4[:, :]).then_inc(s["turned_b"], 1)

                def take_head(j):
                    dve.wait_ge(s["head_made"], head(j))
                    hl = tile_of(mix, turn.at(j, GROUP))
                    dve.tensor_copy(hl[:, 0:TOK], bank7[:, 0:TOK]).then_inc(s["head_rounded"], 1)
                    dve.wait_ge(s["head_rounded"], turn.at(2 * j + 1, 2 * GROUP))
                    dve.tensor_tensor(hl[:, TOK:2 * TOK], bank7[:, 0:TOK], hl[:, 0:TOK].bitcast(F32), ALU.subtract).then_inc(s["head_rounded"], 1)

                def norm_values(j):
                    dve.wait_ge(s["v_turned"], head(j))
                    bank = bank_of(GROUP + 2 * j)
                    dve.tensor_reduce(mv[:, 0, :], bank[:, 0:TOK].rearrange("p (a f) -> p a f", a=2), AX_X,
                                      ALU.add).then_inc(s["v_summed"], 1)
                    dve.wait_ge(s["v_summed"], head(j))
                    dve.tensor_scalar(mv[:, 1, :], mv[:, 0, :], 1.0 / P, None, ALU.mult).then_inc(s["v_mean"], 1)
                    dve.wait_ge(s["v_mean"], head(j))
                    for half in range(2):
                        e = dve.tensor_scalar(vn[:, half, :], bank[:, half * P:(half + 1) * P], mv[:, 1, half:half + 1],
                                              None, ALU.subtract)
                    e.then_inc(s["v_centred"], 1)
                    dve.wait_ge(s["v_std"], head(j))
                    dve.reciprocal(vstd[:, 1, :], vstd[:, 0, :]).then_inc(s["v_recip"], 1)
                    dve.wait_ge(s["v_recip"], head(j))
                    for half in range(2):
                        e = dve.tensor_scalar(vn[:, half, :], vn[:, half, :], vstd[:, 1, half:half + 1], None, ALU.mult)
                    e.then_inc(s["v_normed"], 1)

                def take_group(j):
                    dve.wait_ge(s["g_mixed"], head(j))
                    dve.wait_ge(s["bias_in"], turn.at(16 * (j + 1), 16 * GROUP))
                    bank = bank_of(GROUP + 2 * j)
                    gain = g_gain[:, bass.ds(turn.at(j, GROUP), 1)]
                    dve.scalar_tensor_tensor(cva[:, :].rearrange("p (a t) -> p a t", a=2), bank[:, 0:TOK].rearrange("p (a t) -> p a t", a=2),
                                             gain, g_bias[:, j % 2, :].unsqueeze(1).broadcast_to([P, 2, P]),
                                             ALU.mult, ALU.add).then_inc(s["g_biased"], 1)
                    dve.wait_ge(s["g_biased"], head(j))
                    dve.wait_ge(s["u_gelu"], head(j))
                    dve.tensor_tensor(cvb[:, :], cva[:, :], u_act[:, :], ALU.mult).then_inc(s["g_prod"], 1)
                    dve.wait_ge(s["g_prod"], head(j))
                    split_mix(cvb[:, :], turn.at(HEADS + j, GROUP), head(j)).then_inc(s["mix_split"], 1)

                todo = {1: [(q_inverse, 0)], 2: [(softmax, 0), (q_inverse, 1)], 3: [(q_inverse, 2)],
                        4: [(q_inverse, 3), (copy_turned, 0), (softmax, 1)], 5: [(take_head, 0), (norm_values, 0)],
                        6: [(take_group, 0), (copy_turned, 1), (softmax, 2)], 7: [(take_head, 1), (norm_values, 1)],
                        8: [(take_group, 1), (copy_turned, 2), (softmax, 3)], 9: [(take_head, 2), (norm_values, 2)],
                        10: [(take_group, 2), (copy_turned, 3)], 11: [(take_head, 3), (norm_values, 3), (take_group, 3)]}
                dve.tensor_copy(vtok[:, 0, :, :], vtok[:, bass.ds(turn.at(0, 1), 1), :, :].rearrange("p a n f -> p (a n) f")).then_inc(s["values_placed"], 1)
                for t in range(3 * GROUP):
                    subtract_slab(hd, turn, t, 3 * GROUP)
                    total = sum_chunk(hd, turn, t, 3 * GROUP)
                    if t < GROUP:
                        dve.tensor_tensor(cvc[:, t % 2, :], total, rstd[:, :], ALU.mult).then_inc(s["q_scaled"], 1)
                        dve.wait_ge(s["q_scaled"], head(t))
                        dve.tensor_scalar(qn[:, t, :], cvc[:, t % 2, :], q_gain[:, 1:2], None, ALU.mult).then_inc(s["q_gained"], 1)
                    elif t % 2 == 0:
                        dve.tensor_tensor(scaled[:, :], total, rstd[:, :], ALU.mult).then_inc(s["v_scaled"], 1)
                    else:
                        dve.tensor_tensor(prod[:, :], total, rstd[:, :], ALU.mult).then_inc(s["u_scaled"], 1)
                    for step, j in todo.get(t, []):
                        step(j)

            with dve.Fori(0, KV) as g:
                heads_turn(Turn(g))

            def out_projection(stage, norm, updated):
                def body(turn):
                    for j in range(BANKS):
                        for p in range(stage.per_chunk):
                            subtract_slab(stage, turn, stage.per_chunk * j + p, stage.per_chunk * BANKS)
                        total = sum_chunk(stage, turn, j, BANKS)
                        tile = turn.at(j, BANKS)
                        dve.tensor_tensor(tile_of(x, tile), tile_of(x, tile), total, ALU.add).then_inc(s["x_updated"], 1)
                        dve.wait_ge(s["x_updated"], turn.at(updated + j + 1, BANKS))
                        if norm is not None:
                            split_x(norm, turn, j, BANKS)
                turns(dve, stage, BANKS * stage.per_chunk, body)

            out_projection(STAGES["mix_out"], 1, 0)
            for layer in range(2):
                if layer:
                    inverse_rms(2)
                    st = STAGES["conv_in"]

                    def body(turn):
                        for j in range(12):
                            subtract_slab(st, turn, j, 12)
                            total = sum_chunk(st, turn, j, 12)
                            n, kind = j // 3, j % 3
                            done = turn.at(n + 1, 4)
                            tile = turn.at(n, 4)
                            if kind == 0:
                                dve.tensor_tensor(prod[:, :], total, rstd[:, :], ALU.mult).then_inc(s["c_scaled"], 1)
                            elif kind == 1:
                                dve.tensor_tensor(scaled[:, :], total, rstd[:, :], ALU.mult).then_inc(s["b_in_scaled"], 1)
                                dve.wait_ge(s["c_scaled"], done)
                                dve.wait_ge(s["b_in_scaled"], done)
                                dve.tensor_tensor(gp[:, n % 2, 2:TOK + 2], prod[:, :], scaled[:, :], ALU.mult).then_inc(s["cx_made"], 1)
                                dve.wait_ge(s["cx_made"], done)

                                def weight(tap):
                                    if isinstance(tile, int):
                                        return od_cw[:, tile, tap:tap + 1]
                                    return od_cw[:, bass.ds(tile, 1), tap:tap + 1].rearrange("p a b -> p (a b)")
                                conv3(gp[:, n % 2, :], weight, cvc[:, n % 2, :], turn.at(2 * HALF_FT + n + 1, 4))
                            else:
                                dve.tensor_tensor(scaled[:, :], total, rstd[:, :], ALU.mult).then_inc(s["b_scaled"], 1)
                                dve.wait_ge(s["b_scaled"], done)
                                dve.wait_ge(s["conv_c"], turn.at(2 * HALF_FT + n + 1, 4))
                                dve.tensor_tensor(cva[:, :], cvc[:, n % 2, :], scaled[:, :], ALU.mult).then_inc(s["bc_made"], 1)
                                dve.wait_ge(s["bc_made"], done)
                                split_mix(cva[:, :], tile, turn.at(HEADS + n + 1, 4)).then_inc(s["mix_split"], 1)
                    turns(dve, st, 12, body)
                    out_projection(STAGES["conv_out"], 3, 3 * KT)
                inverse_rms(1 + 2 * layer)
                for half in range(2):
                    st = STAGES["up", layer, half]
                    pair0 = (2 * layer + half) * HALF_FT
                    tile0 = half * HALF_FT

                    def body(turn):
                        for j in range(4):
                            subtract_slab(st, turn, j, 4)
                            total = sum_chunk(st, turn, j, 4)
                            n = j // 2
                            done = turn.at(pair0 + n + 1, 2)
                            f = turn.at(tile0 + n, 2)
                            if j % 2 == 0:
                                dve.tensor_tensor(gp[:, n, 2:TOK + 2], total, rstd[:, :], ALU.mult).then_inc(s["gate_scaled"], 1)
                                dve.wait_ge(s["gate_scaled"], done)

                                def weight(tap):
                                    if isinstance(f, int):
                                        return ffn_cw[:, layer, f, tap:tap + 1]
                                    return ffn_cw[:, layer, bass.ds(f, 1), tap:tap + 1].rearrange("p a b -> p (a b)")
                                conv3(gp[:, n, :], weight, cvc[:, n, :], turn.at(pair0 + KT * layer + n + 1, 2))
                            else:
                                dve.tensor_tensor(scaled[:, :], total, rstd[:, :], ALU.mult).then_inc(s["up_scaled"], 1)
                                dve.wait_ge(s["up_scaled"], done)
                                dve.wait_ge(s["silu_done"], done)
                                dve.tensor_tensor(prod[:, :], scaled[:, :], sil[:, n, :], ALU.mult).then_inc(s["h_made"], 1)
                                dve.wait_ge(s["h_made"], done)
                                hl = tile_of(hidden, turn.at(n, 2))
                                dve.tensor_copy(hl[:, 0:TOK], prod[:, :]).then_inc(s["h_rounded"], 1)
                                dve.wait_ge(s["h_rounded"], done)
                                dve.tensor_tensor(hl[:, TOK:2 * TOK], prod[:, :], hl[:, 0:TOK].bitcast(F32),
                                                  ALU.subtract).then_inc(s["h_split"], 1)
                    turns(dve, st, 4, body)
                    out_projection(STAGES["down", layer, half], 2 if half == 1 and layer == 0 else None,
                                   (1 if layer == 0 else 4) * KT + half * KT)


K_CHUNKS = [4, 5, 8, 9]
V_CHUNKS = [6, 7, 10, 11]
GATE_CHUNK = 12
N_PARAMS = 9
N_CONSTS = 11
N_PADS = 6


def kernel(x, ev_norm, ev_w_in, ev_q_gain, ev_k_gain, ev_cmp_pe, ev_cmp_k_w1, ev_cmp_k_w2, ev_cmp_v_w1, ev_cmp_v_w2,
           ev_gmlp_norm, ev_gmlp_ws, ev_gmlp_b, ev_w_out, od_norm, od_w_in, od_conv_w, od_w_out,
           ffn_norm, ffn_w_in, ffn_conv_w, ffn_conv_b, ffn_w_down):
    import numpy as np
    import concourse.bacc as bacc
    from concourse.bass_utils import run_bass_kernel_spmd

    def slabs(w, tiles):
        w = np.asarray(w)
        n = w.shape[1] // P
        parts = w.shape[0] // (P * tiles)
        return np.ascontiguousarray(
            w.reshape(parts, tiles, P, n, P).transpose(3, 0, 2, 1, 4).reshape(n * parts, P, tiles * P))

    def by_feature(v):
        v = np.asarray(v)
        v = v.reshape(*v.shape[:-1], -1, P)
        return np.ascontiguousarray(np.moveaxis(v, -1, 0))

    w_in = np.asarray(ev_w_in[0])
    q_w = HEADS * P
    kv_w = KV * P
    n_gate = 3 * HEADS
    gate0 = q_w + 6 * kv_w
    g = HEADS * P
    kc, vc, ks, vs, kw, vw = (w_in[:, q_w + n * kv_w:q_w + (n + 1) * kv_w] for n in range(6))
    gate = np.concatenate([w_in[:, gate0:gate0 + n_gate], np.zeros((D_MODEL, P - n_gate), w_in.dtype)], axis=1)
    q = w_in[:, 0:q_w]
    u = w_in[:, gate0 + n_gate:gate0 + n_gate + g]
    v = w_in[:, gate0 + n_gate + g:]
    cols = [kc, vc, ks, vs, kw, vw, gate]
    for grp in range(KV):
        cols.append(q[:, grp * GROUP * P:(grp + 1) * GROUP * P])
        for j in range(grp * GROUP, (grp + 1) * GROUP):
            cols += [v[:, j * P:(j + 1) * P], u[:, j * P:(j + 1) * P]]
    mixer_in = slabs(np.concatenate(cols, axis=1), KT)

    def interleaved(w, parts):
        s = slabs(w, KT)
        n = s.shape[0] // len(parts)
        return np.ascontiguousarray(np.stack([s[a * n:(a + 1) * n] for a in parts], axis=1).reshape(s.shape))

    w1 = np.stack([np.asarray(ev_cmp_k_w1[0]), np.asarray(ev_cmp_v_w1[0])])
    cmp_w1 = np.ascontiguousarray(w1.reshape(4, KT, P, P).transpose(0, 2, 1, 3).reshape(4, P, WIDE))
    down = np.concatenate([slabs(np.asarray(ffn_w_down[layer])[half * HALF_FT * P:(half + 1) * HALF_FT * P], FF_SLAB_TILES)
                           for layer in range(2) for half in range(2)])
    taps = np.concatenate([np.asarray(ffn_conv_w), np.asarray(ffn_conv_b)[:, None, :]], axis=1)
    arrays = {
        "x": np.ascontiguousarray(np.asarray(x)[0].T.reshape(KT, P, TOK)),
        "mixer_in": mixer_in,
        "cmp_w1": cmp_w1,
        "mixer_out": slabs(ev_w_out[0], KT),
        "conv_in": interleaved(od_w_in[0], (1, 2, 0)),
        "conv_out": slabs(od_w_out[0], KT),
        "ffn_up": np.concatenate([interleaved(ffn_w_in[layer], (0, 1)) for layer in range(2)]),
        "ffn_down": down,
        "gains": by_feature(np.stack([np.asarray(ev_norm)[0], np.asarray(ffn_norm)[0], np.asarray(od_norm)[0],
                                      np.asarray(ffn_norm)[1]])),
        "ffn_cw": np.ascontiguousarray(by_feature(taps).transpose(0, 1, 3, 2)),
        "od_cw": np.ascontiguousarray(by_feature(np.asarray(od_conv_w)[0]).transpose(0, 2, 1)),
        "w2k": np.ascontiguousarray(ev_cmp_k_w2[0]),
        "w2v": np.ascontiguousarray(ev_cmp_v_w2[0]),
        "pe": np.ascontiguousarray(np.asarray(ev_cmp_pe)[0].T),
        "q_gain": np.ascontiguousarray(np.asarray(ev_q_gain)[0][:, None]),
        "k_gain": np.ascontiguousarray(np.asarray(ev_k_gain)[0].T),
        "g_gain": np.ascontiguousarray(np.asarray(ev_gmlp_norm)[0].T),
        "ws": np.ascontiguousarray(np.asarray(ev_gmlp_ws)[0].transpose(0, 2, 1)),
        "g_bias": np.ascontiguousarray(ev_gmlp_b[0]),
    }
    nc = bacc.Bacc("TRN2", target_bir_lowering=False, num_devices=1)
    io = {n: nc.dram_tensor(f"in_{n}", a.shape, F32, kind="ExternalInput").ap() for n, a in arrays.items()}
    io["out"] = nc.dram_tensor("out_x", (KT, P, TOK), F32, kind="ExternalOutput").ap()
    build(nc, io)
    r = run_bass_kernel_spmd(nc, [{f"in_{n}": a for n, a in arrays.items()}], core_ids=[0])
    y = r.results[0]["out_x"]
    return np.ascontiguousarray(y.reshape(D_MODEL, TOK).T).reshape(1, TOK, D_MODEL)
```

```python
from contextlib import ExitStack

import concourse.bass as bass
from concourse import mybir

F32 = mybir.dt.float32
F32R = mybir.dt.float32r
ACT = mybir.ActivationFunctionType
ALU = mybir.AluOpType
AX_X = mybir.AxisListType.X

P = 128
TOK = 256
D_MODEL = 2048
KT = D_MODEL // P
D_FF = 5632
FT = D_FF // P
HALF_FT = FT // 2
FF_SLAB_TILES = HALF_FT // 2
HEADS, KV, GROUP = 8, 2, 4
CMP_BLOCK, CMP_STRIDE = 32, 16
N_CMP = (TOK - CMP_BLOCK) // CMP_STRIDE + 1
CMP_PAD = 16
EPS = 1e-6
NEG = -1e30
SMALL = 1e-30

WIDE = KT * P
NARROW = FF_SLAB_TILES * P
AHEAD = 3
AUX_TILE = 13

GATE_CHUNK = 4
K_CHUNKS = [5, 6, 9, 10]
V_CHUNKS = [7, 8, 11, 12]
KV_CHUNKS = 13
FIRST_SLABS = ([("kv", t) for t in range(7)] + [("compress", 0), ("kv", 7), ("compress", 1), ("kv", 8), ("compress", 2), ("kv", 9),
                                                ("compress", 3)] + [("kv", t) for t in range(10, KV_CHUNKS)])
V_SLABS = [4, 6, 8, 9]
U_SLABS = [5, 7, 10, 11]
RING = 4
BANKS = 4


class Stage:

    def __init__(self, before, slabs, width, per_chunk, chunks=None):
        self.slab0 = before.slab0 + before.slabs if before else 0
        self.chunk0 = before.chunk0 + before.chunks if before else 0
        self.slabs, self.width, self.per_chunk = slabs, width, per_chunk
        self.chunks = slabs // per_chunk if chunks is None else chunks


def plan():
    s = {}
    before = None
    for slab in FIRST_SLABS:
        before = s[slab] = Stage(before, 1, WIDE, 1, chunks=int(slab[0] == "kv"))
    s["heads"] = Stage(before, 3 * HEADS, WIDE, 1)
    s["mix_out"] = Stage(s["heads"], KT, WIDE, 1)
    before = s["mix_out"]
    for layer in range(2):
        if layer:
            s["conv_in"] = Stage(before, 3 * KT, WIDE, 1)
            s["conv_out"] = Stage(s["conv_in"], KT, WIDE, 1)
            before = s["conv_out"]
        for half in range(2):
            s["up", layer, half] = Stage(before, 2 * HALF_FT, WIDE, 1)
            s["down", layer, half] = Stage(s["up", layer, half], 2 * KT, NARROW, 2)
            before = s["down", layer, half]
    return s


STAGES = plan()


def width_of(slab):
    for st in STAGES.values():
        if st.slab0 <= slab < st.slab0 + st.slabs:
            return st.width
    return None


class Turn:

    def __init__(self, i=None, k=0):
        self.i, self.k = i, k

    def at(self, base, step):
        return base + step * self.k if self.i is None else self.i * step + base


def wait(eng, sem, value):
    if not isinstance(value, int) or value > 0:
        eng.wait_ge(sem, value)


def build(nc, io):
    with ExitStack() as ctx:
        def sb(name, shape, dt=F32):
            return ctx.enter_context(nc.sbuf_tensor(name, shape, dt))

        def sem(name):
            return ctx.enter_context(nc.semaphore(name))

        raw = sb("raw", [P, RING, WIDE // 2])
        w = sb("w", [P, RING, 2, WIDE], F32R)
        x = sb("x_res", [P, KT, TOK])
        xn = sb("xn", [P, KT, 2 * TOK], F32R)
        lo_part = sb("lo_part", [P, 2, TOK])
        sums = sb("sums", [P, TOK])
        gp = sb("gate_padded", [P, 2, TOK + 2])
        cva = sb("conv_a_buf", [P, TOK])
        cvb = sb("conv_b_buf", [P, TOK])
        cvc = sb("conv_c_buf", [P, 2, TOK])
        sil = sb("silu_buf", [P, 2, TOK])
        scaled = sb("scaled_buf", [P, TOK])
        prod = sb("prod_buf", [P, TOK])
        sq = sb("sq", [P, 2, TOK])
        ssq = sb("ssq", [P, TOK])
        rms = cvb
        rstd = sb("rstd", [P, TOK])
        ones = sb("ones", [P, P])
        ident = sb("ident", [P, P])
        gains = sb("gains", [P, 4, KT])
        ffn_cw = sb("ffn_cw", [P, 2, FT, 4])
        od_cw = sb("od_cw", [P, KT, 3])
        with nc.sbuf_tensor("hidden", [P, HALF_FT, 2 * TOK], F32R) as hidden:
            pass
        mix = sb("mix", [P, KT, 2 * TOK], F32R)
        with nc.sbuf_tensor("kvc", [P, 4, TOK], F32) as kvc:
            pass
        qn = sb("qn", [P, GROUP, TOK])
        kn = sb("kn", [P, 2, KV, TOK])
        vtok = sb("vtok", [P, KV, 5, P])
        with nc.sbuf_tensor("blk", [P, CMP_BLOCK, KV * CMP_PAD], F32) as blk:
            pass
        pt0 = sb("pt0", [P, 2, TOK])
        pt1 = sb("pt1", [P, 4, P])
        p0 = sb("p0", [P, 2, P])
        p1 = sil
        pc = sb("pc", [P, 2, CMP_PAD])
        pcp = sb("pcp", [P, 2, P])
        q_ms = sb("q_ms_buf", [P, GROUP, 2])
        q_r = sb("q_r_buf", [P, GROUP, 2])
        eps_tile = sb("eps_tile", [P, 1])
        stat = sb("stat", [P, 4, 2, 3])
        gates = sb("gates", [P, 2, HEADS, 3])
        kcn = sb("kcn", [P, KV * CMP_PAD])
        hk = sb("hk", [P, KV, CMP_PAD])
        kct = sb("kct", [P, 3, KV * CMP_PAD])
        causal = sb("causal", [P, TOK])
        cmp_neg = sb("cmp_neg", [P, 2, CMP_PAD])
        cmp_keep = sb("cmp_keep", [P, 2, CMP_PAD])
        with nc.sbuf_tensor("w2", [P, 2, P], F32) as w2:
            w2k, w2v = w2[:, 0, :], w2[:, 1, :]
        vn = sb("vn", [P, 2, 2, P])
        with nc.sbuf_tensor("hv", [P, KV, P], F32) as hv:
            pass
        v_act = sb("v_act", [P, TOK])
        pe_t = sb("pe_t", [P, CMP_BLOCK])
        q_gain = sb("q_gain", [P, 2])
        k_gain = sb("k_gain", [P, 3])
        g_gain = sb("g_gain", [P, HEADS])
        ws = sb("ws", [P, 2, P])
        g_bias = sb("g_bias", [P, 2, P])
        u_act = sb("u_act", [P, TOK])
        mv = sb("mv", [P, 2, 2])
        v_var = sb("v_var", [P, 2])
        v_r = sb("v_r", [P, 2])
        minus_half = sb("minus_half", [P, 2])

        acc = [ctx.enter_context(nc.psum_tensor(f"acc{b}", [P, 512], F32)) for b in range(BANKS)]
        bank4, bank5, bank6, bank7 = (ctx.enter_context(nc.psum_tensor(f"bank{b}", [P, 512], F32)) for b in range(4, 8))

        raw_in = [sem(f"raw_in{i}") for i in range(RING)]
        x_in = [sem(f"x_in{i}") for i in range(4)]
        names = """hi_made lo_made slab_used lo_copied chunk_summed
            gains_in x0_rounded params_in x_updated x_squared x_rounded x_split ssq_added norm_summed rms_made rstd_made ssq_cleared
            consts_made pads_made eps_made
            gate_scaled conv_a conv_b conv_c silu_done up_scaled h_made h_rounded h_split
            c_scaled b_in_scaled cx_made b_scaled bc_made mix_rounded mix_split
            kv_scaled k_squared aux_made aux_read k_recip k_normed sig_done
            blk_made blk_rounded blk_split cmp_copied cmp_turned cmp_gelu kc_made kc_copied kc_squared kc_ms kc_rms kc_recip kc_normed vc_made bank7_read mixed_read
            q_gain_made values_placed q_scaled q_squared q_ms_made q_ms_copied q_ms_shifted q_recip q_gained scores_made masked maxed max_scaled exp_done cmp_masked cmp_summed
            sum_floored sum_recip weight_made probs_scaled turned turned_a turned_b head_made head_rounded
            v_scaled v_gelu v_turned v_summed v_mean v_centred v_squared v_var_shifted v_recip v_normed g_mixed u_scaled u_gelu g_prod
            ws_in ws_masked bias_in out_stored""".split()
        s = {n: sem(n) for n in names}

        block = ctx.enter_context(nc.Block())

        def x0_squares(n):
            return (sq[:, :, :], kvc[:, 2:4, :], cvc[:, :, :])[n % 3]

        def ring(slab):
            return slab % RING

        def blk_hl(which):
            n = CMP_BLOCK * 2 * KV * CMP_PAD
            flat = mix[:, :, :].rearrange("p k t -> p (k t)")
            return flat[:, which * n:(which + 1) * n].rearrange("p (l c) -> p l c", l=CMP_BLOCK)

        def ahead_width(stage, turn, slab):
            return stage.width if turn.i is not None else width_of(slab)

        def turns(eng, stage, per_turn, body):
            n = stage.slabs // per_turn
            end = stage.slab0 + stage.slabs
            peel = width_of(end) != stage.width
            with eng.Fori(0, n - peel) as i:
                body(Turn(i))
            if peel:
                body(Turn(None, n - 1))

        def kn_chunk(t):
            i = K_CHUNKS.index(t)
            return kn[:, i // 2, i % 2, :]

        @block.sync
        def _(sp):
            def load_slab(stage, turn, j, src, step, src0, halves=range(2)):
                for half in halves:
                    static = 2 * (stage.slab0 + j) + half
                    slot = static % RING
                    w = stage.width // 2
                    piece = turn.at(static - RING + 1, 2 * step)
                    wait(sp, s["lo_made"], piece)
                    sp.dma_start(raw[:, slot, 0:w], src(turn.at(src0 + j, step), half * w, w)).then_inc(raw_in[slot], 16)

            def load_stage(stage, src, src0=0, loaded=0):
                first = stage.slabs % 2 + (0 if stage.slab0 else RING // 2)
                for j in range(loaded, first):
                    load_slab(stage, Turn(), j, src, 2, src0)
                with sp.Fori(0, (stage.slabs - first) // 2) as i:
                    for j in range(2):
                        load_slab(stage, Turn(i), first + j, src, 2, src0)

            def stream(name):
                t = io[name]

                def src(n, lo, w):
                    if isinstance(n, int):
                        return t[n, :, lo:lo + w]
                    return t[bass.ds(n, 1), :, lo:lo + w].rearrange("a p w -> (a p) w")
                return src

            sp.dma_start(gains[:, :, :], io["gains"]).then_inc(s["gains_in"], 16)
            for quarter in range(4):
                k = KT // 4
                sp.dma_start(x[:, quarter * k:(quarter + 1) * k, :],
                             io["x"][quarter * k:(quarter + 1) * k].rearrange("k p t -> p k t")).then_inc(x_in[quarter], 16)
                if quarter < 2:
                    load_slab(STAGES["kv", 0], Turn(), 0, stream("mixer_in"), 2, 0, [quarter])
            load_stage(Stage(None, len(FIRST_SLABS), WIDE, 1), stream("mixer_in"), loaded=1)
            load_stage(STAGES["heads"], stream("mixer_in"), len(FIRST_SLABS))
            load_stage(STAGES["mix_out"], stream("mixer_out"))
            for layer in range(2):
                if layer:
                    load_stage(STAGES["conv_in"], stream("conv_in"))
                    load_stage(STAGES["conv_out"], stream("conv_out"))
                for half in range(2):
                    load_stage(STAGES["up", layer, half], stream("ffn_up"), (2 * layer + half) * 2 * HALF_FT)
                    load_stage(STAGES["down", layer, half], stream("ffn_down"), (2 * layer + half) * 2 * KT)
            done, pieces = 5 * KT, [0, 4, 8, 12, 14, 15, 16]
            for a, b in zip(pieces, pieces[1:]):
                sp.wait_ge(s["x_updated"], done + b)
                sp.dma_start(io["out"][a:b].rearrange("k p t -> p k t"), x[:, a:b, :]).then_inc(s["out_stored"], 16)
            sp.wait_ge(s["out_stored"], 16 * (len(pieces) - 1))

        @block.gpsimd
        def _(pool):
            n_par = 0
            for dst, name in ((ffn_cw[:, :, :, :], "ffn_cw"), (od_cw[:, :, :], "od_cw"),
                              (w2k, "w2k"), (w2v, "w2v"), (pe_t[:, :], "pe"), (q_gain[:, 0:1], "q_gain"),
                              (k_gain[:, :], "k_gain"), (g_gain[:, :], "g_gain")):
                pool.dma_start(dst, io[name]).then_inc(s["params_in"], 16)
                n_par += 1
            assert n_par == N_PARAMS
            pool.memset(ones[:, :], 1.0).then_inc(s["consts_made"], 1)
            pool.memset(ident[:, :], 1.0).then_inc(s["consts_made"], 1)
            pool.memset(causal[:, :], 0.0).then_inc(s["consts_made"], 1)
            pool.memset(cmp_neg[:, :, :], 0.0).then_inc(s["consts_made"], 1)
            pool.memset(cmp_keep[:, :, :], 1.0).then_inc(s["consts_made"], 1)
            pool.wait_ge(s["consts_made"], 5)
            pool.affine_select(out=ident[:, :], in_=ident[:, :], pattern=[[-1, P]], compare_op=ALU.is_equal,
                               fill=0.0, base=0, channel_multiplier=1).then_inc(s["consts_made"], 1)
            pool.affine_select(out=causal[:, P:TOK], in_=causal[:, P:TOK], pattern=[[-1, P]], compare_op=ALU.is_ge,
                               fill=NEG, base=0, channel_multiplier=1).then_inc(s["consts_made"], 1)
            for half in range(2):
                for dst, fill in ((cmp_neg, NEG), (cmp_keep, 0.0)):
                    pool.affine_select(out=dst[:, half, :], in_=dst[:, half, :], pattern=[[-CMP_STRIDE, CMP_PAD]],
                                       compare_op=ALU.is_ge, fill=fill, base=half * P - (CMP_BLOCK - 1),
                                       channel_multiplier=1).then_inc(s["consts_made"], 1)
            pool.memset(minus_half[:, :], -0.5).then_inc(s["consts_made"], 1)
            pool.wait_ge(s["consts_made"], N_CONSTS)

            def heads_turn(turn):
                def head(j):
                    return turn.at(j + 1, GROUP)

                def query(j):
                    pool.wait_ge(s["q_ms_copied"], head(j))
                    pool.tensor_scalar(q_ms[:, j, :], q_ms[:, j, :], 1.0 / P, EPS, ALU.mult, ALU.add).then_inc(s["q_ms_shifted"], 1)
                    pool.wait_ge(s["q_ms_shifted"], head(j))
                    pool.tensor_tensor(q_r[:, j, :], q_ms[:, j, :], minus_half[:, :], ALU.pow).then_inc(s["q_recip"], 1)

                def values(j):
                    pool.wait_ge(s["v_squared"], head(j))
                    pool.tensor_scalar(v_var[:, :], v_var[:, :], 1.0 / P, EPS, ALU.mult, ALU.add).then_inc(s["v_var_shifted"], 1)
                    pool.wait_ge(s["v_var_shifted"], head(j))
                    pool.tensor_tensor(v_r[:, :], v_var[:, :], minus_half[:, :], ALU.pow).then_inc(s["v_recip"], 1)

                def token_weights(j):
                    b = j % 2
                    pool.wait_ge(s["mixed_read"], turn.at(j, GROUP) if j else turn.at(1, GROUP - 1))
                    g = turn.at(j, GROUP)
                    pool.dma_start(ws[:, b, :], io["ws"][g]).then_inc(s["ws_in"], 16)
                    pool.wait_ge(s["ws_in"], turn.at(16 * (j + 1), 16 * GROUP))
                    pool.dma_start(g_bias[:, b, :], io["g_bias"][g:g + 1, :].broadcast_to([P, P])).then_inc(s["bias_in"], 16)
                    pool.wait_ge(s["bias_in"], turn.at(16 * (j + 1), 16 * GROUP))
                    pool.affine_select(out=ws[:, b, :], in_=ws[:, b, :], pattern=[[1, P]], compare_op=ALU.is_ge,
                                       fill=0.0, base=0, channel_multiplier=-1).then_inc(s["ws_masked"], 1)

                for step, j in ((query, 0), (token_weights, 0), (query, 1), (token_weights, 1), (query, 2), (query, 3),
                                (values, 0), (token_weights, 2), (values, 1), (token_weights, 3), (values, 2), (values, 3)):
                    step(j)

            for g in range(KV):
                heads_turn(Turn(None, g))

        @block.tensor
        def _(pe):
            def tile_products(bank, slot, tile, rhs_hl, n, first, last):
                hi = w[:, slot, 0, tile * P:(tile + 1) * P]
                lo = w[:, slot, 1, tile * P:(tile + 1) * P]
                if last:
                    pe.matmul(bank[:, 0:n], lo, rhs_hl[:, 0:n], start=False, stop=False)
                    return pe.matmul(bank[:, 0:2 * n], hi, rhs_hl, start=first, stop=True)
                pe.matmul(bank[:, 0:2 * n], hi, rhs_hl, start=first, stop=False)
                return pe.matmul(bank[:, 0:n], lo, rhs_hl[:, 0:n], start=False, stop=False)

            def chunk(stage, turn, step, j, rhs, tiles, ready=None, between=None):
                c = stage.chunk0 + j
                bank = acc[c % BANKS]
                wait(pe, s["chunk_summed"], turn.at(c - BANKS + 1, step))
                n = stage.per_chunk
                for part in range(n):
                    slab = stage.slab0 + n * j + part
                    pe.wait_ge(s["lo_made"], turn.at(2 * (slab + 1), 2 * n * step))
                    for t in range(tiles):
                        k = part * tiles + t
                        if ready:
                            ready(k)
                        if between:
                            between(k)
                        mm = tile_products(bank, ring(slab), t, rhs(k), TOK, k == 0, k == n * tiles - 1)
                    mm.then_inc(s["slab_used"], 1)

            def when_x_split(norm):
                def ready(k):
                    if k == 0 and norm:
                        pe.wait_ge(s["x_split"], norm * KT + KT - 4)
                    if k >= KT - 4 or not norm:
                        pe.wait_ge(s["x_split"], norm * KT + k + 1)
                return ready

            def sum_of_squares(norm):
                pe.wait_ge(s["ssq_added"], (norm + 1) * KT)
                if norm == 0:
                    pe.wait_ge(s["consts_made"], N_CONSTS)
                pe.matmul(bank4[:, 0:TOK], ones[:, :], ssq[:, :], start=True, stop=True).then_inc(s["norm_summed"], 1)

            def x_tile(k):
                return xn[:, k, :]

            def mix_tile(k):
                return mix[:, k, :]

            def kv_aux(t):
                bank = acc[t % BANKS]
                if t in K_CHUNKS:
                    pe.wait_ge(s["k_squared"], K_CHUNKS.index(t) + 1)
                    mm = pe.matmul(bank[:, 0:TOK], ones[:, :], sq[:, K_CHUNKS.index(t) % 2, :], start=True, stop=True)
                else:
                    if t in V_CHUNKS:
                        pe.wait_ge(s["kv_scaled"], t + 1)
                        src = cvc[:, V_CHUNKS.index(t) % 2, :]
                    else:
                        pe.wait_ge(s["sig_done"], 1)
                        pe.wait_ge(s["consts_made"], N_CONSTS)
                        src = scaled[:, :]
                    for half in range(2):
                        mm = pe.transpose(bank[:, half * P:(half + 1) * P], src[:, half * P:(half + 1) * P], ident[:, :])
                mm.then_inc(s["aux_made"], 1)

            n_rows = 2 * KV * CMP_PAD

            def compress_slab(n):
                which, part = n // 2, n % 2
                stage = STAGES["compress", n]
                pe.wait_ge(s["blk_split"], which + 1)
                if n == 0:
                    pe.wait_ge(s["rms_made"], 1)
                pe.wait_ge(s["lo_made"], 2 * (stage.slab0 + 1))
                for k in range(KT):
                    pos = part * KT + k
                    mm = pe.matmul((bank4, bank5)[which][0:n_rows, 0:2 * P], blk_hl(which)[:, pos, :],
                                   w[:, ring(stage.slab0), :, k * P:(k + 1) * P], start=pos == 0, stop=pos == CMP_BLOCK - 1)
                mm.then_inc(s["slab_used"], 1)

            def turn_compressed(which):
                pe.wait_ge(s["cmp_copied"], which + 1)
                bank = (bank4, bank5)[which]
                copy = (prod, scaled)[which]
                for part in range(4):
                    columns = copy[0:n_rows, (part % 2) * P:(part % 2 + 1) * P]
                    rows = ident[0:n_rows, (part // 2) * KV * CMP_PAD:(part // 2 + 1) * KV * CMP_PAD]
                    mm = pe.matmul(bank[:, TOK:TOK + KV * CMP_PAD], columns, rows, start=part == 0, stop=part == 3)
                mm.then_inc(s["cmp_turned"], 1)

            def compress_keys():
                pe.wait_ge(s["cmp_gelu"], 1)
                pe.matmul(bank6[:, 0:KV * CMP_PAD], w2k, hk[:, :, :].rearrange("p g n -> p (g n)"),
                          start=True, stop=True).then_inc(s["kc_made"], 1)

            def sum_key_squares():
                pe.wait_ge(s["kc_squared"], 1)
                pe.matmul(bank6[:, 0:KV * CMP_PAD], ones[:, :], kct[:, 1, :], start=True, stop=True).then_inc(s["kc_ms"], 1)

            def compress_values():
                pe.wait_ge(s["cmp_gelu"], 2)
                for g in range(KV):
                    mm = pe.matmul(bank7[:, g * P:(g + 1) * P], hv[:, g, :], w2v, start=True, stop=True)
                mm.then_inc(s["vc_made"], 1)

            todo = {(BANKS - 1, KT // 2): (sum_of_squares, 0), (9, 2): (turn_compressed, 0), (9, 14): (compress_keys,),
                    (10, 9): (turn_compressed, 1), (11, 4): (sum_key_squares,), (11, 8): (compress_values,)}
            for t in range(GATE_CHUNK, KV_CHUNKS - 2):
                todo[t + 2, AUX_TILE] = (kv_aux, t)

            def work(t, k):
                if (t, k) in todo:
                    step, *args = todo[t, k]
                    step(*args)

            for kind, t in FIRST_SLABS:
                if kind == "compress":
                    compress_slab(t)
                    continue
                if t >= 2 * BANKS:
                    pe.wait_ge(s["aux_read"], t - 2 * BANKS + 1)
                chunk(STAGES["kv", t], Turn(), 1, 0, x_tile, KT, when_x_split(0) if t == 0 else None, between=lambda k: work(t, k))
            kv_aux(KV_CHUNKS - 2)
            kv_aux(KV_CHUNKS - 1)
            pe.wait_ge(s["aux_read"], 8)
            pe.wait_ge(s["mixed_read"], 1)

            hd = STAGES["heads"]

            def heads_turn(turn):
                def head(j):
                    return turn.at(j + 1, GROUP)

                def bank_of(t):
                    return acc[(hd.chunk0 + t) % BANKS]

                def mean_square(j):
                    pe.wait_ge(s["q_squared"], head(j))
                    for half in range(2):
                        mm = pe.matmul(bank_of(j)[:, half:half + 1], sq[:, j % 2, half * P:(half + 1) * P], ones[:, 0:1],
                                       start=True, stop=True)
                    mm.then_inc(s["q_ms_made"], 1)

                def scores(j):
                    pe.wait_ge(s["q_gained"], head(j))
                    if j == 0:
                        pe.wait_ge(s["k_normed"], 4)
                        pe.wait_ge(s["kc_normed"], 1)
                    k = [kn[:, b, bass.ds(turn.at(0, 1), 1), :].rearrange("p a t -> p (a t)") for b in range(2)]
                    kc = kcn[:, bass.ds(turn.at(0, CMP_PAD), CMP_PAD)]
                    for half in range(2):
                        q = qn[:, j, half * P:(half + 1) * P]
                        pe.matmul(bank5[:, 256 + half * CMP_PAD:256 + (half + 1) * CMP_PAD], q, kc, start=True, stop=True)
                        for b in range(2):
                            if half == 0:
                                mm = pe.matmul(bank5[:, b * P:(b + 1) * P], q, k[b][:, 0:P], start=True, stop=True)
                            else:
                                mm = pe.matmul(bank6[:, b * TOK:(b + 1) * TOK], q, k[b], start=True, stop=True)
                    mm.then_inc(s["scores_made"], 1)

                def turn_probs(j):
                    pe.wait_ge(s["probs_scaled"], head(j))
                    pe.wait_ge(s["bank7_read"], head(j))
                    for b in range(2):
                        pe.transpose(bank7[:, b * TOK:b * TOK + P], p0[:, b, :], ident[:, :])
                        pe.transpose(bank7[:, b * TOK + P:(b + 1) * TOK], p1[:, b, 0:P], ident[:, :])
                        pe.transpose(bank4[:, b * P:(b + 1) * P], p1[:, b, P:TOK], ident[:, :])
                        mm = pe.transpose(bank4[:, (2 + b) * P:(3 + b) * P], pcp[:, b, :], ident[:, :])
                    mm.then_inc(s["turned"], 1)

                def head_out(j):
                    pe.wait_ge(s["turned_a"], head(j))
                    pe.wait_ge(s["turned_b"], head(j))
                    if j == 0:
                        pe.wait_ge(s["values_placed"], turn.at(1, 1))
                    pe.matmul(bank7[:, 0:TOK], vtok[:, 0, 0, :], pt1[:, 2:4, :].rearrange("p a t -> p (a t)"), start=True, stop=False)
                    for b in range(2):
                        pe.matmul(bank7[:, P:TOK], vtok[:, 0, 2 + 2 * b, :], pt1[:, b, :], start=False, stop=False)
                    for b in range(2):
                        mm = pe.matmul(bank7[:, 0:TOK], vtok[:, 0, 1 + 2 * b, :], pt0[:, b, :], start=False, stop=b == 1)
                    mm.then_inc(s["head_made"], 1)

                def turn_values(j):
                    pe.wait_ge(s["v_gelu"], head(j))
                    bank = bank_of(V_SLABS[j])
                    for half in range(2):
                        mm = pe.transpose(bank[:, half * P:(half + 1) * P], v_act[:, half * P:(half + 1) * P], ident[:, :])
                    mm.then_inc(s["v_turned"], 1)

                def mix_tokens(j):
                    pe.wait_ge(s["v_normed"], head(j))
                    pe.wait_ge(s["ws_masked"], head(j))
                    bank = bank_of(V_SLABS[j])
                    for half in range(2):
                        mm = pe.matmul(bank[:, half * P:(half + 1) * P], vn[:, j % 2, half, :], ws[:, j % 2, :], start=True, stop=True)
                    mm.then_inc(s["g_mixed"], 1)

                todo = {(2, 0): [(mean_square, 0)], (3, 0): [(scores, 0), (mean_square, 1)], (4, 0): [(mean_square, 2)],
                        (5, 0): [(mean_square, 3), (turn_probs, 0), (scores, 1)], (5, 12): [(turn_values, 0)],
                        (6, 0): [(head_out, 0)], (7, 3): [(turn_probs, 1), (scores, 2)],
                        (7, 7): [(mix_tokens, 0)], (7, 12): [(turn_values, 1)], (8, 0): [(head_out, 1)],
                        (9, 6): [(turn_probs, 2), (scores, 3)], (9, 10): [(mix_tokens, 1)],
                        (10, 0): [(head_out, 2)], (10, 2): [(turn_values, 2)], (11, 2): [(turn_values, 3)],
                        (11, 6): [(turn_probs, 3)], (11, 11): [(mix_tokens, 2)], (12, 0): [(head_out, 3), (mix_tokens, 3)]}

                def work(t, k):
                    for step, j in todo.get((t, k), []):
                        step(j)
                for t in range(3 * GROUP):
                    if GROUP <= t < 2 * GROUP:
                        pe.wait_ge(s["q_ms_copied"], head(t - GROUP))
                    work(t, 0)
                    if t - BANKS in V_SLABS:
                        pe.wait_ge(s["mixed_read"], head(V_SLABS.index(t - BANKS) + 1))
                    elif t - BANKS + 3 * GROUP in V_SLABS:
                        pe.wait_ge(s["mixed_read"], turn.at(1, V_SLABS.index(t - BANKS + 3 * GROUP) + 1))
                    chunk(hd, turn, 3 * GROUP, t, x_tile, KT, between=lambda k: k and work(t, k))
                work(3 * GROUP, 0)

            with pe.Fori(0, KV) as g:
                heads_turn(Turn(g))

            def out_projection(stage, split):
                def ready(k):
                    if stage is STAGES["mix_out"] and k == HEADS - 1:
                        pe.wait_ge(s["bank7_read"], 1 + HEADS)
                    if k == 0:
                        pe.wait_ge(s["mix_split"], split + KT - 4)
                    if k >= KT - 4:
                        pe.wait_ge(s["mix_split"], split + k + 1)
                for j in range(BANKS):
                    chunk(stage, Turn(), BANKS, j, mix_tile, KT, ready if j == 0 else None)
                with pe.Fori(1, KT // BANKS) as i:
                    for j in range(BANKS):
                        chunk(stage, Turn(i), BANKS, j, mix_tile, KT)

            pe.wait_ge(s["mixed_read"], 1 + HEADS - 1)
            out_projection(STAGES["mix_out"], HEADS - KT)

            for layer in range(2):
                if layer:
                    st = STAGES["conv_in"]
                    for j in range(12):
                        chunk(st, Turn(), 12, j, x_tile, KT, when_x_split(2) if j == 0 else None)
                        if j == 0:
                            sum_of_squares(2)
                    with pe.Fori(1, st.chunks // 12) as i:
                        for j in range(12):
                            chunk(st, Turn(i), 12, j, x_tile, KT)
                    out_projection(STAGES["conv_out"], HEADS)
                for half in range(2):
                    st = STAGES["up", layer, half]
                    if half == 0:
                        for j in range(BANKS):
                            chunk(st, Turn(), BANKS, j, x_tile, KT, when_x_split(1 + 2 * layer) if j == 0 else None)
                            if j == 0:
                                sum_of_squares(1 + 2 * layer)
                    with pe.Fori(1 - half, st.chunks // BANKS) as i:
                        for j in range(BANKS):
                            chunk(st, Turn(i), BANKS, j, x_tile, KT)
                    st = STAGES["down", layer, half]
                    base = (2 * layer + half) * HALF_FT

                    def ready(k):
                        if k == 0:
                            pe.wait_ge(s["h_split"], base + HALF_FT - 4)
                        if k >= HALF_FT - 4:
                            pe.wait_ge(s["h_split"], base + k + 1)
                    for j in range(BANKS):
                        chunk(st, Turn(), BANKS, j, lambda k: hidden[:, k, :], FF_SLAB_TILES, ready if j == 0 else None)
                    with pe.Fori(1, st.chunks // BANKS) as i:
                        for j in range(BANKS):
                            chunk(st, Turn(i), BANKS, j, lambda k: hidden[:, k, :], FF_SLAB_TILES)

        @block.scalar
        def _(act):
            def round_slab(stage, turn, j, step):
                static = stage.slab0 + j + AHEAD
                slab = turn.at(static, step)
                width = ahead_width(stage, turn, slab)
                if width is None:
                    return
                round_at(turn, static, step, width)

            def round_at(turn, static, step, width):
                h = width // 2
                wait(act, s["slab_used"], turn.at(static - RING + 1, step))
                for half in range(2):
                    piece = 2 * static + half
                    slot = piece % RING
                    act.wait_ge(raw_in[slot], turn.at(16 * (piece // RING + 1), 16 * step // 2))
                    act.activation(w[:, ring(static), 0, half * h:(half + 1) * h], raw[:, slot, 0:h], ACT.Copy).then_inc(s["hi_made"], 1)

            def copy_lo(stage, turn, j, step, per_turn=None):
                c = stage.chunk0 + j
                n = stage.per_chunk
                per = n * step
                act.wait_ge(s["slab_used"], turn.at(stage.slab0 + n * (j + 1), per))
                wait(act, s["chunk_summed"], turn.at(c - 1, step))
                act.activation(lo_part[:, c % 2, :], acc[c % BANKS][:, TOK:2 * TOK], ACT.Copy).then_inc(s["lo_copied"], 1)

            def square_x(first, turn, j, step, updated):
                if updated is not None:
                    act.wait_ge(s["x_updated"], turn.at(updated + j + 1, step))
                wait(act, s["ssq_added"], turn.at(first + j - 1, step))
                tile = turn.at(j, step)
                src = x[:, tile, :] if isinstance(tile, int) else x[:, bass.ds(tile, 1), :].rearrange("p a t -> p (a t)")
                act.activation(sq[:, j % 2, :], src, ACT.Square).then_inc(s["x_squared"], 1)

            def root_mean(norm):
                act.wait_ge(s["norm_summed"], norm + 1)
                act.activation(rms[:, :], bank4[:, 0:TOK], ACT.Sqrt, bias=eps[:, :], scale=1.0 / D_MODEL).then_inc(s["rms_made"], 1)

            act.wait_ge(s["pads_made"], N_PADS)
            eps = eps_tile[:, :]
            act.activation(eps, stat[:, 3, 0, 0:1], ACT.Copy).then_inc(s["eps_made"], 1)
            act.wait_ge(s["eps_made"], 1)
            act.wait_ge(s["gains_in"], 16)
            for n in range(KT):
                if n % 4 == 0:
                    act.wait_ge(x_in[n // 4], 16)
                act.activation(xn[:, n, 0:TOK], x[:, n, :], ACT.Copy, scale=gains[:, 0, n:n + 1]).then_inc(s["x0_rounded"], 1)
                if n == 3:
                    round_at(Turn(), 0, 1, WIDE)
            for a in range(1, AHEAD + 1):
                round_at(Turn(), a, 1, WIDE)
            for n in range(KT // 2):
                wait(act, s["ssq_added"], n - 2)
                act.activation(x0_squares(n), x[:, 2 * n:2 * n + 2, :], ACT.Square).then_inc(s["x_squared"], 2)

            def read_aux(t):
                act.wait_ge(s["aux_made"], t - 3)
                bank = acc[t % BANKS]
                if t in K_CHUNKS:
                    i = K_CHUNKS.index(t)
                    wait(act, s["k_recip"], i)
                    act.activation(sil[:, 0, :], bank[:, 0:TOK], ACT.Sqrt, bias=eps[:, :], scale=1.0 / P).then_inc(s["aux_read"], 1)
                elif t in V_CHUNKS:
                    i = V_CHUNKS.index(t)
                    b, g = i // 2, i % 2
                    last = t == KV_CHUNKS - 1
                    act.activation(vtok[:, g, 1 + 2 * b:3 + 2 * b, :].rearrange("p a t -> p (a t)"), bank[:, 0:TOK],
                                   ACT.Copy).then_inc(s["mixed_read" if last else "aux_read"], 1)
                else:
                    act.activation(gates[:, :, :, :].rearrange("p a h b -> p a (h b)"),
                                   bank[:, 0:TOK].rearrange("p (a c) -> p a c", a=2)[:, :, 0:3 * HEADS],
                                   ACT.Copy).then_inc(s["aux_read"], 1)

            def gelu(which):
                act.wait_ge(s["cmp_turned"], which + 1)
                act.activation((hk, hv)[which][:, :, 0:N_CMP],
                               (bank4, bank5)[which][:, TOK:TOK + KV * CMP_PAD].rearrange("p (g n) -> p g n", g=KV)[:, :, 0:N_CMP],
                               ACT.Gelu_apprx_tanh).then_inc(s["cmp_gelu"], 1)

            for kind, t in FIRST_SLABS:
                stage = STAGES[kind, t]
                if stage.slab0 > 0:
                    round_slab(stage, Turn(), 0, 1)
                if kind == "compress":
                    if t % 2:
                        which = t // 2
                        act.wait_ge(s["slab_used"], stage.slab0 + 1)
                        act.activation((prod, scaled)[which][0:2 * KV * CMP_PAD, :],
                                       (bank4, bank5)[which][0:2 * KV * CMP_PAD, 0:TOK], ACT.Copy).then_inc(s["cmp_copied"], 1)
                    continue
                if t == 1:
                    root_mean(0)
                if t - 2 >= GATE_CHUNK:
                    read_aux(t - 2)
                if t == 9:
                    gelu(0)
                elif t == 10:
                    gelu(1)
                    act.wait_ge(s["kc_copied"], 1)
                    act.activation(kct[:, 1, :], kct[:, 0, :], ACT.Square).then_inc(s["kc_squared"], 1)
                elif t == 11:
                    act.wait_ge(s["kc_ms"], 1)
                    act.activation(kct[:, 2, :], bank6[:, 0:KV * CMP_PAD], ACT.Sqrt, bias=eps[:, :], scale=1.0 / P).then_inc(s["kc_rms"], 1)
                    act.wait_ge(s["vc_made"], 1)
                    act.activation(vtok[:, :, 0, :], bank7[:, 0:KV * P].rearrange("p (g f) -> p g f", g=KV), ACT.Copy).then_inc(s["bank7_read"], 1)
                copy_lo(stage, Turn(), 0, 1)
                if t in K_CHUNKS:
                    i = K_CHUNKS.index(t)
                    act.wait_ge(s["kv_scaled"], t + 1)
                    if i >= 2:
                        act.wait_ge(s["aux_made"], K_CHUNKS[i - 2] - 3)
                    act.activation(sq[:, i % 2, :], kn_chunk(t), ACT.Square).then_inc(s["k_squared"], 1)
                if t == GATE_CHUNK:
                    act.wait_ge(s["kv_scaled"], t + 1)
                    act.activation(scaled[:, :], prod[:, :], ACT.Sigmoid).then_inc(s["sig_done"], 1)
            read_aux(KV_CHUNKS - 2)
            read_aux(KV_CHUNKS - 1)

            hd = STAGES["heads"]

            def heads_turn(turn):
                def head(j):
                    return turn.at(j + 1, GROUP)

                def bank_of(t):
                    return acc[(hd.chunk0 + t) % BANKS]

                def copy_mean_square(j):
                    act.wait_ge(s["q_ms_made"], head(j))
                    act.activation(q_ms[:, j, :], bank_of(j)[:, 0:2], ACT.Copy).then_inc(s["q_ms_copied"], 1)

                def exponentials(j):
                    act.wait_ge(s["max_scaled"], head(j))
                    for half in range(2):
                        act.activation(pc[:, half, :], pc[:, half, :], ACT.Exp, bias=stat[:, 1, half, 0:1],
                                       scale=q_r[:, j, half:half + 1])
                        for b in range(2):
                            src = (p0, p1)[half][:, b, :]
                            e = act.activation(src, src, ACT.Exp, bias=stat[:, 1, half, 1 + b:2 + b],
                                               scale=q_r[:, j, half:half + 1], accum_out=stat[:, 2, half, 1 + b:2 + b])
                    e.then_inc(s["exp_done"], 1)

                def copy_turned(j):
                    act.wait_ge(s["turned"], head(j))
                    act.activation(pt0[:, :, :].rearrange("p b t -> p (b t)"), bank7[:, :], ACT.Copy).then_inc(s["turned_a"], 1)

                def square_values(j):
                    act.wait_ge(s["v_centred"], head(j))
                    for half in range(2):
                        e = act.activation(sq[:, 0, half * P:(half + 1) * P], vn[:, j % 2, half, :], ACT.Square,
                                           accum_out=v_var[:, half:half + 1])
                    e.then_inc(s["v_squared"], 1)

                before_epilogue = {3: [(exponentials, 0)], 5: [(exponentials, 1)], 6: [(square_values, 0)], 7: [(exponentials, 2)],
                                   8: [(square_values, 1)], 9: [(exponentials, 3)], 10: [(square_values, 2)], 11: [(square_values, 3)]}
                after_epilogue = {1: [(copy_mean_square, 0)], 2: [(copy_mean_square, 1)], 3: [(copy_mean_square, 2)],
                                  4: [(copy_mean_square, 3), (copy_turned, 0)], 6: [(copy_turned, 1)], 8: [(copy_turned, 2)],
                                  10: [(copy_turned, 3)]}
                for t in range(3 * GROUP):
                    round_slab(hd, turn, t, 3 * GROUP)
                    for step, j in before_epilogue.get(t, []):
                        step(j)
                    copy_lo(hd, turn, t, 3 * GROUP)
                    if t < GROUP:
                        act.wait_ge(s["q_scaled"], head(t))
                        if t >= 2:
                            act.wait_ge(s["q_ms_made"], head(t - 2))
                        act.activation(sq[:, t % 2, :], cvc[:, t % 2, :], ACT.Square).then_inc(s["q_squared"], 1)
                    elif t in V_SLABS:
                        j = V_SLABS.index(t)
                        act.wait_ge(s["v_scaled"], head(j))
                        if j == GROUP - 1:
                            act.wait_ge(s["v_turned"], head(j - 1))
                        act.activation(v_act[:, :], scaled[:, :], ACT.Gelu_apprx_tanh).then_inc(s["v_gelu"], 1)
                    else:
                        j = U_SLABS.index(t)
                        act.wait_ge(s["u_scaled"], head(j))
                        if j == GROUP - 1:
                            act.wait_ge(s["g_prod"], head(j - 1))
                        act.activation(u_act[:, :], prod[:, :], ACT.Gelu_apprx_tanh).then_inc(s["u_gelu"], 1)
                    for step, j in after_epilogue.get(t, []):
                        step(j)

            with act.Fori(0, KV) as g:
                heads_turn(Turn(g))

            def out_projection(stage, norm, updated):
                def body(turn):
                    for j in range(BANKS):
                        for p in range(stage.per_chunk):
                            round_slab(stage, turn, stage.per_chunk * j + p, stage.per_chunk * BANKS)
                        copy_lo(stage, turn, j, BANKS)
                        if norm is not None:
                            square_x(norm * KT, turn, j, BANKS, updated)
                turns(act, stage, BANKS * stage.per_chunk, body)

            out_projection(STAGES["mix_out"], 1, 0)
            for layer in range(2):
                if layer:
                    root_mean(2)
                    st = STAGES["conv_in"]

                    def body(turn):
                        for j in range(12):
                            round_slab(st, turn, j, 12)
                            copy_lo(st, turn, j, 12)
                    turns(act, st, 12, body)
                    out_projection(STAGES["conv_out"], 3, 3 * KT)
                root_mean(1 + 2 * layer)
                for half in range(2):
                    st = STAGES["up", layer, half]
                    pair0 = (2 * layer + half) * HALF_FT
                    tile0 = half * HALF_FT

                    def body(turn):
                        for j in range(4):
                            round_slab(st, turn, j, 4)
                            copy_lo(st, turn, j, 4)
                            if j % 2:
                                act.wait_ge(s["conv_c"], turn.at(pair0 + KT * layer + j // 2 + 1, 2))
                                f = turn.at(tile0 + j // 2, 2)
                                bias = ffn_cw[:, layer, f, 3:4] if isinstance(f, int) else \
                                    ffn_cw[:, layer, bass.ds(f, 1), 3:4].rearrange("p a b -> p (a b)")
                                act.activation(sil[:, j // 2, :], cvc[:, j // 2, :], ACT.Silu, bias=bias).then_inc(s["silu_done"], 1)
                    turns(act, st, 4, body)
                    out_projection(STAGES["down", layer, half], 2 if half == 1 and layer == 0 else None,
                                   (1 if layer == 0 else 4) * KT + half * KT)

        @block.vector
        def _(dve):
            def subtract_slab(stage, turn, j, step):
                static = stage.slab0 + j + AHEAD
                width = ahead_width(stage, turn, turn.at(static, step))
                if width is not None:
                    subtract_at(turn, static, step, width)

            def subtract_at(turn, static, step, width):
                h = width // 2
                for half in range(2):
                    piece = 2 * static + half
                    dve.wait_ge(s["hi_made"], turn.at(piece + 1, 2 * step))
                    part = slice(half * h, (half + 1) * h)
                    dve.tensor_tensor(w[:, ring(static), 1, part], raw[:, piece % RING, 0:h],
                                      w[:, ring(static), 0, part].bitcast(F32), ALU.subtract).then_inc(s["lo_made"], 1)
                if half:
                    dve.wait_ge(s["lo_made"], turn.at(2 * static + 1, 2 * step))

            def sum_chunk(stage, turn, j, step, dst=sums[:, :]):
                c = stage.chunk0 + j
                dve.wait_ge(s["lo_copied"], turn.at(c + 1, step))
                dve.tensor_tensor(dst, acc[c % BANKS][:, 0:TOK], lo_part[:, c % 2, :], ALU.add).then_inc(s["chunk_summed"], 1)
                dve.wait_ge(s["chunk_summed"], turn.at(c + 1, step))
                return dst

            def tile_of(t, tile):
                return t[:, tile, :] if isinstance(tile, int) else t[:, bass.ds(tile, 1), :].rearrange("p a t -> p (a t)")

            def split_x(norm, turn, j, step):
                first = norm * KT + j
                tile = turn.at(j, step)
                gain = tile_of(gains[:, norm, :].rearrange("p (k a) -> p k a", a=1), tile)
                hl = tile_of(xn, tile)
                dve.tensor_scalar(hl[:, 0:TOK], tile_of(x, tile), gain, None, ALU.mult).then_inc(s["x_rounded"], 1)
                dve.wait_ge(s["x_rounded"], turn.at(first + 1 - KT, step))
                dve.scalar_tensor_tensor(hl[:, TOK:2 * TOK], tile_of(x, tile), gain, hl[:, 0:TOK].bitcast(F32),
                                         ALU.mult, ALU.subtract).then_inc(s["x_split"], 1)
                add_square(norm, turn, j, step)

            def add_square(norm, turn, j, step):
                first = norm * KT + j
                dve.wait_ge(s["x_squared"], turn.at(first + 1, step))
                wait(dve, s["ssq_added"], turn.at(first, step))
                dve.tensor_tensor(ssq[:, :], ssq[:, :], sq[:, j % 2, :], ALU.add).then_inc(s["ssq_added"], 1)

            def inverse_rms(norm):
                dve.wait_ge(s["rms_made"], norm + 1)
                dve.reciprocal(rstd[:, :], rms[:, :]).then_inc(s["rstd_made"], 1)
                dve.memset(ssq[:, :], 0.0).then_inc(s["ssq_cleared"], 1)
                dve.wait_ge(s["rstd_made"], norm + 1)
                dve.wait_ge(s["ssq_cleared"], norm + 1)

            def conv3(src, weight, dst, done):
                dve.tensor_scalar(cva[:, :], src[:, 2:TOK + 2], weight(2), None, ALU.mult).then_inc(s["conv_a"], 1)
                dve.wait_ge(s["conv_a"], done)
                dve.scalar_tensor_tensor(cvb[:, :], src[:, 1:TOK + 1], weight(1), cva[:, :], ALU.mult, ALU.add).then_inc(s["conv_b"], 1)
                dve.wait_ge(s["conv_b"], done)
                dve.scalar_tensor_tensor(dst, src[:, 0:TOK], weight(0), cvb[:, :], ALU.mult, ALU.add).then_inc(s["conv_c"], 1)

            dve.memset(gp[:, :, 0:2], 0.0).then_inc(s["pads_made"], 1)
            dve.memset(hk[:, :, :], 0.0).then_inc(s["pads_made"], 1)
            dve.memset(hv[:, :, :], 0.0).then_inc(s["pads_made"], 1)
            dve.memset(blk[:, :, :], 0.0).then_inc(s["pads_made"], 1)
            dve.memset(pcp[:, :, :], 0.0).then_inc(s["pads_made"], 1)
            dve.memset(stat[:, 3, :, :], EPS).then_inc(s["pads_made"], 1)
            dve.wait_ge(s["pads_made"], N_PADS)
            for n in range(KT):
                dve.wait_ge(s["x0_rounded"], n + 1)
                dve.scalar_tensor_tensor(xn[:, n, TOK:2 * TOK], x[:, n, :], gains[:, 0, n:n + 1],
                                         xn[:, n, 0:TOK].bitcast(F32), ALU.mult, ALU.subtract).then_inc(s["x_split"], 1)
                if n == 3:
                    subtract_at(Turn(), 0, 1, WIDE)
            for a in range(1, AHEAD + 1):
                subtract_at(Turn(), a, 1, WIDE)
            for n in range(KT // 2):
                dve.wait_ge(s["x_squared"], 2 * (n + 1))
                if n == 0:
                    dve.tensor_copy(kvc[:, 0:2, :], x0_squares(n)).then_inc(s["ssq_added"], 1)
                else:
                    dve.wait_ge(s["ssq_added"], n)
                    dve.tensor_tensor(kvc[:, 0:2, :], kvc[:, 0:2, :], x0_squares(n), ALU.add).then_inc(s["ssq_added"], 1)
            dve.wait_ge(s["ssq_added"], KT // 2)
            dve.tensor_tensor(ssq[:, :], kvc[:, 0, :], kvc[:, 1, :], ALU.add).then_inc(s["ssq_added"], KT // 2)
            dve.wait_ge(s["ssq_added"], KT)
            dve.wait_ge(s["params_in"], 16 * N_PARAMS)
            dve.wait_ge(s["consts_made"], N_CONSTS)
            dve.tensor_scalar(q_gain[:, 1:2], q_gain[:, 0:1], float(P) ** -0.5, None, ALU.mult).then_inc(s["q_gain_made"], 1)
            dve.wait_ge(s["q_gain_made"], 1)

            def after_aux(t):
                if t in K_CHUNKS:
                    i = K_CHUNKS.index(t)
                    dve.wait_ge(s["aux_read"], t - 3)
                    dve.reciprocal(sil[:, 1, :], sil[:, 0, :]).then_inc(s["k_recip"], 1)
                    dve.wait_ge(s["k_recip"], i + 1)
                    b = i // 2
                    dve.scalar_tensor_tensor(kn_chunk(t), kn_chunk(t), k_gain[:, 1 + b:2 + b], sil[:, 1, :],
                                             ALU.mult, ALU.mult).then_inc(s["k_normed"], 1)

            def make_blocks(which):
                src = kvc[:, 2 * which:2 * which + 2, :].rearrange("p g (m b) -> p b g m", b=CMP_STRIDE)
                for a in range(2):
                    dst = blk[:, a * CMP_STRIDE:(a + 1) * CMP_STRIDE, :].rearrange("p l (g n) -> p l g n", g=KV)[:, :, :, 0:N_CMP]
                    pos = pe_t[:, a * CMP_STRIDE:(a + 1) * CMP_STRIDE].unsqueeze(2).unsqueeze(3)
                    dve.tensor_tensor(dst, src[:, :, :, a:a + N_CMP], pos.broadcast_to([P, CMP_STRIDE, KV, N_CMP]),
                                      ALU.add).then_inc(s["blk_made"], 1)

            def split_blocks(which):
                n = KV * CMP_PAD
                dve.wait_ge(s["blk_made"], 2 * (which + 1))
                dve.tensor_copy(blk_hl(which)[:, :, 0:n], blk[:, :, :]).then_inc(s["blk_rounded"], 1)
                dve.wait_ge(s["blk_rounded"], which + 1)
                dve.tensor_tensor(blk_hl(which)[:, :, n:2 * n], blk[:, :, :], blk_hl(which)[:, :, 0:n].bitcast(F32),
                                  ALU.subtract).then_inc(s["blk_split"], 1)

            for kind, t in FIRST_SLABS:
                stage = STAGES[kind, t]
                if stage.slab0 > 0:
                    subtract_slab(stage, Turn(), 0, 1)
                if kind == "compress":
                    continue
                if t - 2 in K_CHUNKS:
                    after_aux(t - 2)
                if t == 10:
                    dve.wait_ge(s["kc_made"], 1)
                    dve.tensor_copy(kct[:, 0, :], bank6[:, 0:KV * CMP_PAD]).then_inc(s["kc_copied"], 1)
                total = sum_chunk(stage, Turn(), 0, 1, kvc[:, 0, :] if t == 0 else sums[:, :])
                if t == 0:
                    continue
                if t == 1:
                    inverse_rms(0)
                    dve.tensor_tensor(kvc[:, 0, :], kvc[:, 0, :], rstd[:, :], ALU.mult).then_inc(s["kv_scaled"], 1)
                if t < 4:
                    dst = kvc[:, t, :]
                elif t in K_CHUNKS:
                    dst = kn_chunk(t)
                elif t in V_CHUNKS:
                    dst = cvc[:, V_CHUNKS.index(t) % 2, :]
                else:
                    dst = prod[:, :]
                if t in V_CHUNKS and V_CHUNKS.index(t) >= 2:
                    dve.wait_ge(s["aux_made"], V_CHUNKS[V_CHUNKS.index(t) - 2] - 3)
                dve.tensor_tensor(dst, total, rstd[:, :], ALU.mult).then_inc(s["kv_scaled"], 1)
                if t in (2, 5):
                    make_blocks(t // 3)
                if t in (3, 6):
                    split_blocks(t // 4)

            dve.wait_ge(s["kc_rms"], 1)
            dve.reciprocal(kcn[:, :], kct[:, 2, :]).then_inc(s["kc_recip"], 1)
            dve.wait_ge(s["kc_recip"], 1)
            dve.scalar_tensor_tensor(kcn[:, :], kct[:, 0, :], k_gain[:, 0:1], kcn[:, :], ALU.mult, ALU.mult).then_inc(s["kc_normed"], 1)
            dve.wait_ge(s["bank7_read"], 1)
            dve.wait_ge(s["mixed_read"], 1)

            hd = STAGES["heads"]

            def split_mix(src, tile, count):
                hl = tile_of(mix, tile)
                dve.tensor_copy(hl[:, 0:TOK], src).then_inc(s["mix_rounded"], 1)
                dve.wait_ge(s["mix_rounded"], count)
                return dve.tensor_tensor(hl[:, TOK:2 * TOK], src, hl[:, 0:TOK].bitcast(F32), ALU.subtract)

            def heads_turn(turn):
                def head(j):
                    return turn.at(j + 1, GROUP)

                def bank_of(t):
                    return acc[(hd.chunk0 + t) % BANKS]

                def mask_and_max(j):
                    dve.wait_ge(s["scores_made"], head(j))
                    dve.wait_ge(s["q_recip"], head(j))
                    dve.tensor_tensor(p0[:, :, :], bank5[:, 0:2 * P].rearrange("p (b t) -> p b t", b=2),
                                      causal[:, P:TOK].unsqueeze(1).broadcast_to([P, 2, P]), ALU.add).then_inc(s["masked"], 1)
                    dve.tensor_tensor(p1[:, :, :], bank6[:, :].rearrange("p (b t) -> p b t", b=2),
                                      causal[:, :].unsqueeze(1).broadcast_to([P, 2, TOK]), ALU.add).then_inc(s["masked"], 1)
                    dve.tensor_tensor(pc[:, :, :], bank5[:, 2 * P:2 * P + 2 * CMP_PAD].rearrange("p (b t) -> p b t", b=2),
                                      cmp_neg[:, :, :], ALU.add).then_inc(s["masked"], 1)
                    dve.wait_ge(s["masked"], turn.at(3 * (j + 1), 3 * GROUP))
                    dve.tensor_reduce(stat[:, 0, 0, 1:3], p0[:, :, :], AX_X, ALU.max, negate=True).then_inc(s["maxed"], 1)
                    dve.tensor_reduce(stat[:, 0, 1, 1:3], p1[:, :, :], AX_X, ALU.max, negate=True).then_inc(s["maxed"], 1)
                    dve.tensor_reduce(stat[:, 0, :, 0:1].rearrange("p a b -> p (a b)"), pc[:, :, :], AX_X, ALU.max, negate=True).then_inc(s["maxed"], 1)
                    dve.wait_ge(s["maxed"], turn.at(3 * (j + 1), 3 * GROUP))
                    dve.scalar_tensor_tensor(stat[:, 1, :, :], stat[:, 0, :, :], -NEG / 10, q_r[:, j, :].unsqueeze(2).broadcast_to([P, 2, 3]),
                                             ALU.min, ALU.mult).then_inc(s["max_scaled"], 1)

                def weigh(j):
                    dve.wait_ge(s["exp_done"], head(j))
                    dve.tensor_tensor(pc[:, :, :], pc[:, :, :], cmp_keep[:, :, :], ALU.mult).then_inc(s["cmp_masked"], 1)
                    dve.wait_ge(s["cmp_masked"], head(j))
                    dve.tensor_reduce(stat[:, 2, :, 0:1].rearrange("p a b -> p (a b)"), pc[:, :, :], AX_X, ALU.add).then_inc(s["cmp_summed"], 1)
                    dve.wait_ge(s["cmp_summed"], head(j))
                    dve.tensor_scalar(stat[:, 0, :, :], stat[:, 2, :, :], SMALL, None, ALU.max).then_inc(s["sum_floored"], 1)
                    dve.wait_ge(s["sum_floored"], head(j))
                    dve.reciprocal(stat[:, 1, :, :], stat[:, 0, :, :]).then_inc(s["sum_recip"], 1)
                    dve.wait_ge(s["sum_recip"], head(j))
                    gate = gates[:, :, bass.ds(turn.at(j, GROUP), 1), :].rearrange("p a h b -> p a (h b)")
                    dve.tensor_tensor(stat[:, 0, :, :], stat[:, 1, :, :], gate, ALU.mult).then_inc(s["weight_made"], 1)
                    dve.wait_ge(s["weight_made"], head(j))
                    for half in range(2):
                        dve.tensor_scalar(pcp[:, half, 0:CMP_PAD], pc[:, half, :], stat[:, 0, half, 0:1], None, ALU.mult)
                        for b in range(2):
                            src = (p0, p1)[half][:, b, :]
                            e = dve.tensor_scalar(src, src, stat[:, 0, half, 1 + b:2 + b], None, ALU.mult)
                    e.then_inc(s["probs_scaled"], 1)

                def copy_turned(j):
                    dve.wait_ge(s["turned"], head(j))
                    dve.tensor_copy(pt1[:, :, :].rearrange("p b t -> p (b t)"), bank4[:, :]).then_inc(s["turned_b"], 1)

                def take_head(j):
                    dve.wait_ge(s["head_made"], head(j))
                    hl = tile_of(mix, turn.at(j, GROUP))
                    dve.tensor_copy(hl[:, 0:TOK], bank7[:, 0:TOK]).then_inc(s["head_rounded"], 1)
                    dve.wait_ge(s["head_rounded"], head(j))
                    dve.tensor_tensor(hl[:, TOK:2 * TOK], bank7[:, 0:TOK], hl[:, 0:TOK].bitcast(F32), ALU.subtract).then_inc(s["bank7_read"], 1)

                def centre_values(j):
                    dve.wait_ge(s["v_turned"], head(j))
                    bank = bank_of(V_SLABS[j])
                    dve.tensor_reduce(mv[:, 0, :], bank[:, 0:TOK].rearrange("p (a f) -> p a f", a=2), AX_X,
                                      ALU.add).then_inc(s["v_summed"], 1)
                    dve.wait_ge(s["v_summed"], head(j))
                    dve.tensor_scalar(mv[:, 1, :], mv[:, 0, :], 1.0 / P, None, ALU.mult).then_inc(s["v_mean"], 1)
                    dve.wait_ge(s["v_mean"], head(j))
                    for half in range(2):
                        e = dve.tensor_scalar(vn[:, j % 2, half, :], bank[:, half * P:(half + 1) * P], mv[:, 1, half:half + 1],
                                              None, ALU.subtract)
                    e.then_inc(s["v_centred"], 1)

                def divide_values(j):
                    dve.wait_ge(s["v_recip"], head(j))
                    for half in range(2):
                        e = dve.tensor_scalar(vn[:, j % 2, half, :], vn[:, j % 2, half, :], v_r[:, half:half + 1], None, ALU.mult)
                    e.then_inc(s["v_normed"], 1)

                def take_group(j):
                    dve.wait_ge(s["g_mixed"], head(j))
                    dve.wait_ge(s["bias_in"], turn.at(16 * (j + 1), 16 * GROUP))
                    bank = bank_of(V_SLABS[j])
                    gain = g_gain[:, bass.ds(turn.at(j, GROUP), 1)]
                    dve.scalar_tensor_tensor(cva[:, :].rearrange("p (a t) -> p a t", a=2), bank[:, 0:TOK].rearrange("p (a t) -> p a t", a=2),
                                             gain, g_bias[:, j % 2, :].unsqueeze(1).broadcast_to([P, 2, P]),
                                             ALU.mult, ALU.add).then_inc(s["mixed_read"], 1)
                    dve.wait_ge(s["mixed_read"], head(j + 1))
                    dve.wait_ge(s["u_gelu"], head(j))
                    dve.tensor_tensor(cvb[:, :], cva[:, :], u_act[:, :], ALU.mult).then_inc(s["g_prod"], 1)
                    dve.wait_ge(s["g_prod"], head(j))
                    split_mix(cvb[:, :], turn.at(HEADS + j, GROUP), head(j)).then_inc(s["mix_split"], 1)

                before_sum = {6: [(divide_values, 0)], 8: [(divide_values, 1)], 10: [(divide_values, 2)], 11: [(divide_values, 3), (take_group, 2)]}
                after_sum = {2: [(mask_and_max, 0)], 3: [(weigh, 0)],
                             4: [(copy_turned, 0), (mask_and_max, 1)], 5: [(weigh, 1), (take_head, 0), (centre_values, 0)],
                             6: [(copy_turned, 1), (take_group, 0), (mask_and_max, 2)], 7: [(weigh, 2), (take_head, 1), (centre_values, 1)],
                             8: [(copy_turned, 2), (take_group, 1), (mask_and_max, 3)], 9: [(weigh, 3), (take_head, 2), (centre_values, 2)],
                             10: [(copy_turned, 3), (centre_values, 3)], 11: [(take_head, 3), (take_group, 3)]}
                dve.tensor_copy(vtok[:, 0, :, :], vtok[:, bass.ds(turn.at(0, 1), 1), :, :].rearrange("p a n f -> p (a n) f")).then_inc(s["values_placed"], 1)
                for t in range(3 * GROUP):
                    subtract_slab(hd, turn, t, 3 * GROUP)
                    for step, j in before_sum.get(t, []):
                        step(j)
                    total = sum_chunk(hd, turn, t, 3 * GROUP)
                    if t < GROUP:
                        dve.tensor_tensor(cvc[:, t % 2, :], total, rstd[:, :], ALU.mult).then_inc(s["q_scaled"], 1)
                        dve.wait_ge(s["q_scaled"], head(t))
                        dve.tensor_scalar(qn[:, t, :], cvc[:, t % 2, :], q_gain[:, 1:2], None, ALU.mult).then_inc(s["q_gained"], 1)
                    elif t in V_SLABS:
                        dve.tensor_tensor(scaled[:, :], total, rstd[:, :], ALU.mult).then_inc(s["v_scaled"], 1)
                    else:
                        dve.tensor_tensor(prod[:, :], total, rstd[:, :], ALU.mult).then_inc(s["u_scaled"], 1)
                    for step, j in after_sum.get(t, []):
                        step(j)

            with dve.Fori(0, KV) as g:
                heads_turn(Turn(g))

            def out_projection(stage, norm, updated):
                def body(turn):
                    for j in range(BANKS):
                        for p in range(stage.per_chunk):
                            subtract_slab(stage, turn, stage.per_chunk * j + p, stage.per_chunk * BANKS)
                        total = sum_chunk(stage, turn, j, BANKS)
                        tile = turn.at(j, BANKS)
                        dve.tensor_tensor(tile_of(x, tile), tile_of(x, tile), total, ALU.add).then_inc(s["x_updated"], 1)
                        dve.wait_ge(s["x_updated"], turn.at(updated + j + 1, BANKS))
                        if norm is not None:
                            split_x(norm, turn, j, BANKS)
                turns(dve, stage, BANKS * stage.per_chunk, body)

            out_projection(STAGES["mix_out"], 1, 0)
            for layer in range(2):
                if layer:
                    inverse_rms(2)
                    st = STAGES["conv_in"]

                    def body(turn):
                        for j in range(12):
                            subtract_slab(st, turn, j, 12)
                            total = sum_chunk(st, turn, j, 12)
                            n, kind = j // 3, j % 3
                            done = turn.at(n + 1, 4)
                            tile = turn.at(n, 4)
                            if kind == 0:
                                dve.tensor_tensor(prod[:, :], total, rstd[:, :], ALU.mult).then_inc(s["c_scaled"], 1)
                            elif kind == 1:
                                dve.tensor_tensor(scaled[:, :], total, rstd[:, :], ALU.mult).then_inc(s["b_in_scaled"], 1)
                                dve.wait_ge(s["c_scaled"], done)
                                dve.wait_ge(s["b_in_scaled"], done)
                                dve.tensor_tensor(gp[:, n % 2, 2:TOK + 2], prod[:, :], scaled[:, :], ALU.mult).then_inc(s["cx_made"], 1)
                                dve.wait_ge(s["cx_made"], done)

                                def weight(tap):
                                    if isinstance(tile, int):
                                        return od_cw[:, tile, tap:tap + 1]
                                    return od_cw[:, bass.ds(tile, 1), tap:tap + 1].rearrange("p a b -> p (a b)")
                                conv3(gp[:, n % 2, :], weight, cvc[:, n % 2, :], turn.at(2 * HALF_FT + n + 1, 4))
                            else:
                                dve.tensor_tensor(scaled[:, :], total, rstd[:, :], ALU.mult).then_inc(s["b_scaled"], 1)
                                dve.wait_ge(s["b_scaled"], done)
                                dve.wait_ge(s["conv_c"], turn.at(2 * HALF_FT + n + 1, 4))
                                dve.tensor_tensor(cva[:, :], cvc[:, n % 2, :], scaled[:, :], ALU.mult).then_inc(s["bc_made"], 1)
                                dve.wait_ge(s["bc_made"], done)
                                split_mix(cva[:, :], tile, turn.at(HEADS + n + 1, 4)).then_inc(s["mix_split"], 1)
                    turns(dve, st, 12, body)
                    out_projection(STAGES["conv_out"], 3, 3 * KT)
                inverse_rms(1 + 2 * layer)
                for half in range(2):
                    st = STAGES["up", layer, half]
                    pair0 = (2 * layer + half) * HALF_FT
                    tile0 = half * HALF_FT

                    def body(turn):
                        for j in range(4):
                            subtract_slab(st, turn, j, 4)
                            total = sum_chunk(st, turn, j, 4)
                            n = j // 2
                            done = turn.at(pair0 + n + 1, 2)
                            f = turn.at(tile0 + n, 2)
                            if j % 2 == 0:
                                dve.tensor_tensor(gp[:, n, 2:TOK + 2], total, rstd[:, :], ALU.mult).then_inc(s["gate_scaled"], 1)
                                dve.wait_ge(s["gate_scaled"], done)

                                def weight(tap):
                                    if isinstance(f, int):
                                        return ffn_cw[:, layer, f, tap:tap + 1]
                                    return ffn_cw[:, layer, bass.ds(f, 1), tap:tap + 1].rearrange("p a b -> p (a b)")
                                conv3(gp[:, n, :], weight, cvc[:, n, :], turn.at(pair0 + KT * layer + n + 1, 2))
                            else:
                                dve.tensor_tensor(scaled[:, :], total, rstd[:, :], ALU.mult).then_inc(s["up_scaled"], 1)
                                dve.wait_ge(s["up_scaled"], done)
                                dve.wait_ge(s["silu_done"], done)
                                dve.tensor_tensor(prod[:, :], scaled[:, :], sil[:, n, :], ALU.mult).then_inc(s["h_made"], 1)
                                dve.wait_ge(s["h_made"], done)
                                hl = tile_of(hidden, turn.at(n, 2))
                                dve.tensor_copy(hl[:, 0:TOK], prod[:, :]).then_inc(s["h_rounded"], 1)
                                dve.wait_ge(s["h_rounded"], done)
                                dve.tensor_tensor(hl[:, TOK:2 * TOK], prod[:, :], hl[:, 0:TOK].bitcast(F32),
                                                  ALU.subtract).then_inc(s["h_split"], 1)
                    turns(dve, st, 4, body)
                    out_projection(STAGES["down", layer, half], 2 if half == 1 and layer == 0 else None,
                                   (1 if layer == 0 else 4) * KT + half * KT)


N_PARAMS = 8
N_CONSTS = 12
N_PADS = 6


def kernel(x, ev_norm, ev_w_in, ev_q_gain, ev_k_gain, ev_cmp_pe, ev_cmp_k_w1, ev_cmp_k_w2, ev_cmp_v_w1, ev_cmp_v_w2,
           ev_gmlp_norm, ev_gmlp_ws, ev_gmlp_b, ev_w_out, od_norm, od_w_in, od_conv_w, od_w_out,
           ffn_norm, ffn_w_in, ffn_conv_w, ffn_conv_b, ffn_w_down):
    import numpy as np
    import concourse.bacc as bacc
    from concourse.bass_utils import run_bass_kernel_spmd

    def slabs(w, tiles):
        w = np.asarray(w)
        n = w.shape[1] // P
        parts = w.shape[0] // (P * tiles)
        return np.ascontiguousarray(
            w.reshape(parts, tiles, P, n, P).transpose(3, 0, 2, 1, 4).reshape(n * parts, P, tiles * P))

    def by_feature(v):
        v = np.asarray(v)
        v = v.reshape(*v.shape[:-1], -1, P)
        return np.ascontiguousarray(np.moveaxis(v, -1, 0))

    w_in = np.asarray(ev_w_in[0])
    q_w = HEADS * P
    kv_w = KV * P
    n_gate = 3 * HEADS
    gate0 = q_w + 6 * kv_w
    g = HEADS * P
    kc, vc, ks, vs, kw, vw = (w_in[:, q_w + n * kv_w:q_w + (n + 1) * kv_w] for n in range(6))
    gate = np.concatenate([w_in[:, gate0:gate0 + n_gate], np.zeros((D_MODEL, P - n_gate), w_in.dtype)], axis=1)
    q = w_in[:, 0:q_w]
    u = w_in[:, gate0 + n_gate:gate0 + n_gate + g]
    v = w_in[:, gate0 + n_gate + g:]
    cols = [kc, vc, gate, ks, vs, kw, vw]
    for grp in range(KV):
        cols.append(q[:, grp * GROUP * P:(grp + 1) * GROUP * P])
        for t in range(GROUP, 3 * GROUP):
            part, j = (v, V_SLABS.index(t)) if t in V_SLABS else (u, U_SLABS.index(t))
            j += grp * GROUP
            cols.append(part[:, j * P:(j + 1) * P])
    mixer_in = slabs(np.concatenate(cols, axis=1), KT)

    def interleaved(w, parts):
        s = slabs(w, KT)
        n = s.shape[0] // len(parts)
        return np.ascontiguousarray(np.stack([s[a * n:(a + 1) * n] for a in parts], axis=1).reshape(s.shape))

    w1 = np.stack([np.asarray(ev_cmp_k_w1[0]), np.asarray(ev_cmp_v_w1[0])])
    cmp_w1 = np.ascontiguousarray(w1.reshape(4, KT, P, P).transpose(0, 2, 1, 3).reshape(4, P, WIDE))
    first = [mixer_in[t] if kind == "kv" else cmp_w1[t] for kind, t in FIRST_SLABS]
    mixer_in = np.concatenate([np.stack(first), mixer_in[KV_CHUNKS:]])
    down = np.concatenate([slabs(np.asarray(ffn_w_down[layer])[half * HALF_FT * P:(half + 1) * HALF_FT * P], FF_SLAB_TILES)
                           for layer in range(2) for half in range(2)])
    taps = np.concatenate([np.asarray(ffn_conv_w), np.asarray(ffn_conv_b)[:, None, :]], axis=1)
    arrays = {
        "x": np.ascontiguousarray(np.asarray(x)[0].T.reshape(KT, P, TOK)),
        "mixer_in": mixer_in,
        "mixer_out": slabs(ev_w_out[0], KT),
        "conv_in": interleaved(od_w_in[0], (1, 2, 0)),
        "conv_out": slabs(od_w_out[0], KT),
        "ffn_up": np.concatenate([interleaved(ffn_w_in[layer], (0, 1)) for layer in range(2)]),
        "ffn_down": down,
        "gains": by_feature(np.stack([np.asarray(ev_norm)[0], np.asarray(ffn_norm)[0], np.asarray(od_norm)[0],
                                      np.asarray(ffn_norm)[1]])),
        "ffn_cw": np.ascontiguousarray(by_feature(taps).transpose(0, 1, 3, 2)),
        "od_cw": np.ascontiguousarray(by_feature(np.asarray(od_conv_w)[0]).transpose(0, 2, 1)),
        "w2k": np.ascontiguousarray(ev_cmp_k_w2[0]),
        "w2v": np.ascontiguousarray(ev_cmp_v_w2[0]),
        "pe": np.ascontiguousarray(np.asarray(ev_cmp_pe)[0].T),
        "q_gain": np.ascontiguousarray(np.asarray(ev_q_gain)[0][:, None]),
        "k_gain": np.ascontiguousarray(np.asarray(ev_k_gain)[0].T),
        "g_gain": np.ascontiguousarray(np.asarray(ev_gmlp_norm)[0].T),
        "ws": np.ascontiguousarray(np.asarray(ev_gmlp_ws)[0].transpose(0, 2, 1)),
        "g_bias": np.ascontiguousarray(ev_gmlp_b[0]),
    }
    nc = bacc.Bacc("TRN2", target_bir_lowering=False, num_devices=1)
    io = {n: nc.dram_tensor(f"in_{n}", a.shape, F32, kind="ExternalInput").ap() for n, a in arrays.items()}
    io["out"] = nc.dram_tensor("out_x", (KT, P, TOK), F32, kind="ExternalOutput").ap()
    build(nc, io)
    r = run_bass_kernel_spmd(nc, [{f"in_{n}": a for n, a in arrays.items()}], core_ids=[0])
    y = r.results[0]["out_x"]
    return np.ascontiguousarray(y.reshape(D_MODEL, TOK).T).reshape(1, TOK, D_MODEL)
```
